# Optimizing a Trainium2 kernel written in Bass

```python
import math
import jax
import jax.numpy as jnp
from jax import lax
import numpy as np

D_MODEL = 2048
BATCH = 1
SEQ = 256
DEPTH = 1

CHUNK = 64
SSM_EXPAND = 2
D_INNER = SSM_EXPAND * D_MODEL
SSM_HEAD_DIM = 64
SSM_HEADS = D_INNER // SSM_HEAD_DIM
SSM_GROUPS = 8
SSM_STATE = 128
CONV_K = 4
CONV_DIM = D_INNER + 2 * SSM_GROUPS * SSM_STATE
ATT_HEAD_DIM = 64
ATT_HEADS = D_MODEL // ATT_HEAD_DIM
ATT_KV_HEADS = 8
WINDOW = 128
WINDOW_CHUNKS = WINDOW // CHUNK
REL_BUCKETS = 32
REL_MAX_DIST = 128
D_FF = 4 * D_MODEL
EPS = 1e-6

Z_OFF = 0
XBC_OFF = Z_OFF + D_INNER
DT_OFF = XBC_OFF + CONV_DIM
Q_OFF = DT_OFF + SSM_HEADS
K_OFF = Q_OFF + ATT_HEADS * ATT_HEAD_DIM
V_OFF = K_OFF + ATT_KV_HEADS * ATT_HEAD_DIM
GA_OFF = V_OFF + ATT_KV_HEADS * ATT_HEAD_DIM
GB_OFF = GA_OFF + D_MODEL
IN_COLS = GB_OFF + D_MODEL

kernel_name = 'hybrid_ssd_swa_sink_encoder'

def _rmsnorm(x, w):
    x32 = x.astype(jnp.float32)
    y = x32 * lax.rsqrt(jnp.mean(x32 * x32, axis=-1, keepdims=True) + EPS)
    return (y * w.astype(jnp.float32)).astype(x.dtype)

def _gated_group_rmsnorm(y, z, w):
    b, t, _ = y.shape
    g = (y * jax.nn.silu(z)).astype(jnp.float32).reshape(b, t, SSM_GROUPS, -1)
    g = g * lax.rsqrt(jnp.mean(g * g, axis=-1, keepdims=True) + EPS)
    return (g.reshape(b, t, -1) * w.astype(jnp.float32)).astype(y.dtype)

def _causal_depthwise_conv(u, w, bias):
    out = lax.conv_general_dilated(
        u, w[:, None, :].astype(u.dtype), window_strides=(1,),
        padding=[(CONV_K - 1, 0)], dimension_numbers=('NWC', 'WIO', 'NWC'),
        feature_group_count=u.shape[-1])
    return out + bias.astype(u.dtype)

def _t5_bucket(rel):
    nb = REL_BUCKETS // 2
    ret = (rel > 0).astype(np.int32) * nb
    n = np.abs(rel)
    max_exact = nb // 2
    large = max_exact + (np.log(np.maximum(n, 1) / max_exact)
                         / np.log(REL_MAX_DIST / max_exact) * (nb - max_exact)).astype(np.int32)
    large = np.minimum(large, nb - 1)
    return (ret + np.where(n < max_exact, n, large)).astype(np.int32)

def _shift_chunks(t, n):
    if n == 0:
        return t
    nc = t.shape[1]
    pad = [(0, 0)] * t.ndim
    pad[1] = (n, 0)
    return jnp.pad(t, pad)[:, :nc]

def _ssd(xh, dt, A, Bm, Cm, d_skip):
    b, T, H, P = xh.shape
    L = CHUNK
    nc = T // L
    G = SSM_GROUPS
    E = H // G
    N = Bm.shape[-1]
    x_ = xh.reshape(b, nc, L, G, E, P)
    dt_ = dt.reshape(b, nc, L, G, E)
    Bc = Bm.reshape(b, nc, L, G, N)
    Cc = Cm.reshape(b, nc, L, G, N)
    a = dt_ * A.reshape(G, E)
    a_cs = jnp.cumsum(jnp.moveaxis(a, 2, -1), axis=-1)
    xdt = x_ * dt_[..., None]
    causal = np.tril(np.ones((L, L), dtype=bool))
    seg = a_cs[..., :, None] - a_cs[..., None, :]
    decay = jnp.exp(jnp.where(causal, seg, -jnp.inf))
    cb = jnp.einsum('bclgn,bcsgn->bcgls', Cc, Bc)
    y_diag = jnp.einsum('bcgls,bcgels,bcsgep->bclgep', cb, decay, xdt)

    def step(state, inp):
        B_c, C_c, xdt_c, acs_c = inp
        y_off = jnp.einsum('blgn,bgepn,bgel->blgep', C_c, state, jnp.exp(acs_c))
        w_end = jnp.exp(acs_c[..., -1:] - acs_c)
        state = (state * jnp.exp(acs_c[..., -1])[..., None, None]
                 + jnp.einsum('blgn,bgel,blgep->bgepn', B_c, w_end, xdt_c))
        return state, y_off

    init = jnp.zeros((b, G, E, P, N), jnp.float32)
    mv = lambda t: jnp.moveaxis(t, 1, 0)
    _, y_off = lax.scan(step, init, (mv(Bc), mv(Cc), mv(xdt), mv(a_cs)))
    y = y_diag + jnp.moveaxis(y_off, 0, 1) + x_ * d_skip.reshape(G, E)[:, :, None]
    return y.reshape(b, T, H * P)

def _swa_sinks(q, k, v, sinks, rel_bias):
    b, T, _ = q.shape
    L = CHUNK
    nc = T // L
    W = WINDOW_CHUNKS
    KV = ATT_KV_HEADS
    G = ATT_HEADS // KV
    d = ATT_HEAD_DIM
    qc = q.reshape(b, nc, L, KV, G, d)
    kc = k.reshape(b, nc, L, KV, d)
    vc = v.reshape(b, nc, L, KV, d)
    k_band = jnp.concatenate([_shift_chunks(kc, W - 1 - i) for i in range(W)], axis=2)
    v_band = jnp.concatenate([_shift_chunks(vc, W - 1 - i) for i in range(W)], axis=2)
    s = jnp.einsum('bcqkgd,bcskd->bckgqs', qc, k_band).astype(jnp.float32) * (d ** -0.5)
    s = s + rel_bias
    key_chunk = np.arange(nc)[:, None] - (W - 1) + np.arange(W * L)[None, :] // L
    valid = key_chunk >= 0
    s = jnp.where(valid[None, :, None, None, None, :], s, -jnp.inf)
    sink = sinks.astype(jnp.float32).reshape(KV, G)[None, None, :, :, None]
    m = jnp.maximum(s.max(axis=-1), sink)
    p = jnp.exp(s - m[..., None])
    denom = p.sum(axis=-1) + jnp.exp(sink - m)
    probs = (p / denom[..., None]).astype(v.dtype)
    o = jnp.einsum('bckgqs,bcskd->bcqkgd', probs, v_band)
    return o.reshape(b, T, KV * G * d)

def setup_inputs(seed: int = 0) -> dict:
    key = jax.random.key(seed)
    ks = jax.random.split(key, 20)
    f32 = jnp.float32

    def nrm(k, shape, fan_in):
        return jax.random.normal(k, shape, f32) * (fan_in ** -0.5)

    x = jax.random.normal(ks[0], (BATCH, SEQ, D_MODEL), f32)
    rel_table = jax.random.normal(ks[1], (REL_BUCKETS, ATT_HEADS), f32) * 0.5
    norm1_w = 1.0 + 0.05 * jax.random.normal(ks[2], (DEPTH, D_MODEL), f32)
    w_in = nrm(ks[3], (DEPTH, D_MODEL, IN_COLS), D_MODEL)
    conv_w = nrm(ks[4], (DEPTH, CONV_K, CONV_DIM), CONV_K)
    conv_b = 0.02 * jax.random.normal(ks[5], (DEPTH, CONV_DIM), f32)
    dt0 = jnp.exp(jax.random.uniform(ks[6], (DEPTH, SSM_HEADS), f32,
                                     math.log(1e-3), math.log(1e-1)))
    dt_bias = dt0 + jnp.log(-jnp.expm1(-dt0))
    a_log = jnp.log(jax.random.uniform(ks[7], (DEPTH, SSM_HEADS), f32, 1.0, 16.0))
    d_skip = 1.0 + 0.05 * jax.random.normal(ks[8], (DEPTH, SSM_HEADS), f32)
    ssm_norm_w = 1.0 + 0.05 * jax.random.normal(ks[9], (DEPTH, D_INNER), f32)
    sinks = 0.5 * jax.random.normal(ks[10], (DEPTH, ATT_HEADS), f32)
    w_proj_ssm = nrm(ks[11], (DEPTH, D_INNER, D_MODEL), D_INNER)
    w_proj_attn = nrm(ks[12], (DEPTH, ATT_HEADS * ATT_HEAD_DIM, D_MODEL), ATT_HEADS * ATT_HEAD_DIM)
    w_out = nrm(ks[13], (DEPTH, D_MODEL, D_MODEL), D_MODEL)
    norm2_w = 1.0 + 0.05 * jax.random.normal(ks[14], (DEPTH, D_MODEL), f32)
    w_up = nrm(ks[15], (DEPTH, D_MODEL, D_FF), D_MODEL)
    w_down = nrm(ks[16], (DEPTH, D_FF, D_MODEL), D_FF)
    final_norm_w = 1.0 + 0.05 * jax.random.normal(ks[17], (D_MODEL,), f32)
    return {'x': x, 'rel_table': rel_table, 'norm1_w': norm1_w, 'w_in': w_in,
            'conv_w': conv_w, 'conv_b': conv_b, 'dt_bias': dt_bias, 'a_log': a_log,
            'd_skip': d_skip, 'ssm_norm_w': ssm_norm_w, 'sinks': sinks,
            'w_proj_ssm': w_proj_ssm, 'w_proj_attn': w_proj_attn, 'w_out': w_out,
            'norm2_w': norm2_w, 'w_up': w_up, 'w_down': w_down,
            'final_norm_w': final_norm_w}

def reference(x, rel_table, norm1_w, w_in, conv_w, conv_b, dt_bias, a_log, d_skip,
              ssm_norm_w, sinks, w_proj_ssm, w_proj_attn, w_out, norm2_w, w_up,
              w_down, final_norm_w):
    b, T, _ = x.shape
    G, N = SSM_GROUPS, SSM_STATE
    qi = np.arange(CHUNK)[:, None]
    sj = np.arange(WINDOW_CHUNKS * CHUNK)[None, :]
    rel = sj - (WINDOW_CHUNKS - 1) * CHUNK - qi
    buckets = _t5_bucket(rel)
    rel_bias = rel_table[buckets].astype(jnp.float32)
    rel_bias = jnp.transpose(rel_bias, (2, 0, 1)).reshape(
        ATT_KV_HEADS, ATT_HEADS // ATT_KV_HEADS, CHUNK, WINDOW_CHUNKS * CHUNK)

    h = x
    for layer in range(DEPTH):
        u = _rmsnorm(h, norm1_w[layer])
        proj = u @ w_in[layer]
        z = proj[..., Z_OFF:XBC_OFF]
        xbc = proj[..., XBC_OFF:DT_OFF]
        dt_raw = proj[..., DT_OFF:Q_OFF]
        q = proj[..., Q_OFF:K_OFF]
        k = proj[..., K_OFF:V_OFF]
        v = proj[..., V_OFF:GA_OFF]
        gate_a = proj[..., GA_OFF:GB_OFF]
        gate_b = proj[..., GB_OFF:IN_COLS]

        xbc = jax.nn.silu(_causal_depthwise_conv(xbc, conv_w[layer], conv_b[layer]))
        xs = xbc[..., :D_INNER].reshape(b, T, SSM_HEADS, SSM_HEAD_DIM)
        Bm = xbc[..., D_INNER:D_INNER + G * N].reshape(b, T, G, N)
        Cm = xbc[..., D_INNER + G * N:].reshape(b, T, G, N)
        dt = jax.nn.softplus(dt_raw.astype(jnp.float32) + dt_bias[layer].astype(jnp.float32))
        A = -jnp.exp(a_log[layer].astype(jnp.float32))
        y_ssm = _ssd(xs, dt, A, Bm, Cm, d_skip[layer]).astype(h.dtype)
        y_ssm = _gated_group_rmsnorm(y_ssm, z, ssm_norm_w[layer])

        y_att = _swa_sinks(q, k, v, sinks[layer], rel_bias).astype(h.dtype)

        merged = (jax.nn.sigmoid(gate_a) * (y_ssm @ w_proj_ssm[layer])
                  + jax.nn.sigmoid(gate_b) * (y_att @ w_proj_attn[layer]))
        h = h + merged @ w_out[layer]

        u = _rmsnorm(h, norm2_w[layer])
        h = h + jnp.square(jax.nn.relu(u @ w_up[layer])) @ w_down[layer]

    return _rmsnorm(h, final_norm_w)


_drawn_inputs = setup_inputs


def setup_inputs(seed=0):
    import zlib

    import numpy as np

    out = dict(_drawn_inputs(seed))
    spreads = {}
    factors = {'conv_b': 4.045, 'd_skip': 9.565, 'sinks': 8.0}
    for name, (base, spread) in spreads.items():
        noise = np.random.default_rng([zlib.crc32(name.encode()), seed]).standard_normal(out[name].shape)
        drawn = base * np.exp(spread * noise) if base else spread * noise
        out[name] = jnp.asarray(drawn.astype(out[name].dtype))
    for name, factor in factors.items():
        out[name] = (out[name] * factor).astype(out[name].dtype)
    return out
```

```python
from contextlib import ExitStack

import numpy as np
import concourse.bass as bass
from concourse import mybir

F32 = mybir.dt.float32
F32R = mybir.dt.float32r
ALU = mybir.AluOpType
ACT = mybir.ActivationFunctionType
AX = mybir.AxisListType

P = 128
T = 256
TB = T // P
D = 2048
DI = 4096
L = 64
NCH = T // L
SSM_H, SSM_G, NST = 64, 8, 128
HPG = SSM_H // SSM_G
ATT_H, KV, HD = 32, 8, 64
WIN = 2 * L
BUCKETS, MAX_DIST = 32, 128
DFF = 8192
EPS = 1e-6

Z_OFF = 0
XBC_OFF = DI
CONV_DIM = DI + 2 * SSM_G * NST
DT_OFF = XBC_OFF + CONV_DIM
Q_OFF = DT_OFF + SSM_H
K_OFF = Q_OFF + ATT_H * HD
V_OFF = K_OFF + KV * HD
GA_OFF = V_OFF + KV * HD
GB_OFF = GA_OFF + D
IN_COLS = GB_OFF + D

CW = 512
KT = D // P
KPU = 2
UPC = KT // KPU
RING = 4
UE = KPU * CW
MASKED = -1.0e30

CONV_T = CONV_DIM // P
C_CONVW = 0
C_CONVB = C_CONVW + 4 * CONV_T
C_N1 = C_CONVB + CONV_T
C_N2 = C_N1 + KT
C_SSMN = C_N2 + KT
C_SKIP = C_SSMN + DI // P
C_SINK = C_SKIP + DI // P
C_DTB = C_SINK + ATT_H
C_ALOG = C_DTB + 1
C_ALL = C_ALOG + 1
K_ID = 0
K_MASK = K_ID + P
SW = 3 * P
K_ONES = K_MASK + SW
K_ALL = K_ONES + P
LINE = 192


class Lin:

    def __init__(self, c, terms=()):
        self.c, self.terms = c, tuple(terms)

    def __add__(self, k):
        return Lin(self.c + k, self.terms)

    def along(self, coef, reg):
        return Lin(self.c, self.terms + ((coef, reg),))

    def over(self, d):
        assert all(k % d == 0 for k, _ in self.terms)
        return Lin(self.c // d, [(k // d, r) for k, r in self.terms])

    def times(self, m):
        return Lin(self.c * m, [(k * m, r) for k, r in self.terms])

    def mod(self, d):
        assert all(k % d == 0 for k, _ in self.terms)
        return self.c % d

    def val(self):
        v = self.c
        for k, r in self.terms:
            v = r * k + v
        return v


def at(base, step, i):
    return Lin(base + step * i) if isinstance(i, int) else Lin(base).along(step, i)


def cut_at_off(i, size, off):
    return slice(off + i * size, off + (i + 1) * size) if isinstance(i, int) else bass.ds(i * size + off, size)


def cut_at(i, size):
    return slice(i * size, (i + 1) * size) if isinstance(i, int) else bass.ds(i * size, size)


class Chunk:

    def __init__(self, unit, units, number):
        self.unit = unit
        self.units = units
        self.end = unit + units
        self.bank = number.mod(2)
        self.turn = number.over(2)
        self.left = self.turn + 1


DT_UNITS = 2
U_K = DT_UNITS
U_V, U_BC = U_K + UPC, U_K + 2 * UPC
U_Q = U_BC + 4 * UPC
U_X = U_Q + 4 * UPC
U_MERGE = U_X + 18 * UPC
MERGE_U = 5 * UPC
U_OUT = U_MERGE + 4 * MERGE_U - 2 * UPC
U_MLP = U_OUT + 4 * UPC
HALF_U = 8 * UPC + 4 * 2 * UPC
N_BC, N_Q, N_X, N_MERGE, N_OUT, N_MLP, HALF_N = 2, 6, 10, 28, 42, 46, 12

K_CHUNK, V_CHUNK = Chunk(Lin(U_K), UPC, Lin(0)), Chunk(Lin(U_V), UPC, Lin(1))


def q_chunk(j):
    return Chunk(at(U_Q, UPC, j), UPC, at(N_Q, 1, j))


def bc_chunk(j):
    return Chunk(at(U_BC, UPC, j), UPC, at(N_BC, 1, j))


def x_chunk(g):
    return Chunk(at(U_X, 2 * UPC, g), UPC, at(N_X, 2, g))


def z_chunk(g):
    return Chunk(at(U_X + UPC, 2 * UPC, g), UPC, at(N_X + 1, 2, g))


def ga_chunk(j):
    return Chunk(at(U_MERGE - 2 * UPC, MERGE_U, j), UPC, at(N_MERGE - 2, 4, j))


def gb_chunk(j):
    return Chunk(at(U_MERGE - UPC, MERGE_U, j), UPC, at(N_MERGE - 1, 4, j))


def ssm_chunk(j):
    return Chunk(at(U_MERGE, MERGE_U, j), 2 * UPC, at(N_MERGE, 4, j))


def att_chunk(j):
    return Chunk(at(U_MERGE + 2 * UPC, MERGE_U, j), UPC, at(N_MERGE + 1, 4, j))


def is_last(g):
    return isinstance(g, int) and g == SSM_G - 1


def next_x(g):
    return Chunk(at(U_X + 2 * UPC, 2 * UPC, g), UPC, at(N_X + 2, 2, g))


def next_z(g):
    return Chunk(at(U_X + 3 * UPC, 2 * UPC, g), UPC, at(N_X + 3, 2, g))


def part(steps, first):
    return {place - first: run for place, run in steps.items() if first <= place < first + UPC}


def joined(a, b):
    return {u: a.get(u, []) + b.get(u, []) for u in sorted({*a, *b})}


def next_ga(j):
    return Chunk(at(U_MERGE + 3 * UPC, MERGE_U, j), UPC, at(N_MERGE + 2, 4, j))


def next_gb(j):
    return Chunk(at(U_MERGE + 4 * UPC, MERGE_U, j), UPC, at(N_MERGE + 3, 4, j))


def out_chunk(j):
    return Chunk(Lin(U_OUT + j * UPC), UPC, Lin(N_OUT + j))


def up_chunk(half, j, pair=None):
    unit = Lin(U_MLP + j * UPC).along(HALF_U, half)
    number = Lin(N_MLP + j).along(HALF_N, half)
    if pair is not None:
        unit, number = unit.along(2 * UPC, pair), number.along(2, pair)
    return Chunk(unit, UPC, number)


def down_chunk(half, j):
    return Chunk(Lin(U_MLP + (8 + 2 * j) * UPC).along(HALF_U, half), 2 * UPC, Lin(N_MLP + 8 + j).along(HALF_N, half))


def build(nc, x, w_in, w_ssm, w_att, w_out, w_up, w_down, rel_table, fnorm, cols_in, consts_in, onehot_in, out):
    decay_rows = nc.dram_tensor("decay_rows", (2, SSM_H, SW), F32).ap()
    bias_skew = nc.dram_tensor("bias_skew", (ATT_H, L, LINE), F32).ap()

    ctx = ExitStack()
    with ctx:
        def sb(name, shape, dt=F32, stack=ctx):
            return stack.enter_context(nc.sbuf_tensor(name, shape, dt))

        def sem(name):
            return ctx.enter_context(nc.semaphore(name))

        raw = sb("raw", [P, RING, UE])
        w_hi = sb("w_hi", [P, RING, UE], F32R)
        w_lo = sb("w_lo", [P, RING, UE], F32R)
        st_hi = sb("st_hi", [P, KT, T], F32R)
        st_lo = sb("st_lo", [P, KT, T], F32R)
        cols = sb("cols", [P, C_ALL])
        consts = sb("consts", [P, K_ALL])
        stat = sb("stat", [P, 16])
        ident = consts[:, K_ID:K_ID + P]
        mask = consts[:, K_MASK:K_MASK + SW]
        ones = consts[:, K_ONES:K_ONES + P]

        mix = ExitStack()
        y32 = sb("y32", [P, 32, T], stack=mix)
        qatt = sb("qatt", [P, KT, T], stack=mix)
        kdup = sb("kdup", [P, KV, L + T], stack=mix)
        v_win = sb("v_win", [P, NCH, CW], stack=mix)
        bias_g = sb("bias_g", [P, 4, WIN], stack=mix)
        cbm = sb("cbm", [P, SSM_G, SW], stack=mix)
        dec = [sb(f"dec{n}", [P, 4, SW], stack=mix) for n in range(2)]
        xraw = sb("xraw", [P, 4, 3 + T], stack=mix)
        xc = sb("xc", [P, 4, T], stack=mix)
        x_fm = sb("x_fm", [P, 4, T], stack=mix)
        xdt = sb("xdt", [P, TB, CW], stack=mix)
        probs = sb("probs", [P, TB, CW], stack=mix)
        probsT = sb("probsT", [P, TB, CW], stack=mix)
        tmcols = sb("tmcols", [P, 4, SSM_H], stack=mix)
        q_g = sb("q_g", [P, 2, T], stack=mix)
        k_g = sb("k_g", [P, L + T], stack=mix)
        v_g = sb("v_g", [P, NCH, HD], stack=mix)
        cb_g = sb("cb_g", [P, SW], stack=mix)
        smx = sb("smx", [P, 5, 8], stack=mix)
        mix.close()
        x_tm = y32[:, 0:16, :].rearrange("p (b j) t -> p b (j t)", b=TB)
        bc = y32[:, 0:16, :]
        dtw = y32[0:SSM_H, 16:32, :]
        line_sb = y32[0:ATT_H, 31, 0:LINE]
        relt_sb = y32[0:BUCKETS, 30, 0:ATT_H]
        onehot_sb = y32[0:BUCKETS, 30, ATT_H:ATT_H + LINE]
        zs = xc
        sq = xdt[:, :, :].rearrange("p b (j t) -> p (b j) t", t=T)
        ms_g, rstd_g = sq[:, 2, :], sq[:, 3, :]

        mrg = ExitStack()
        y_lo = sb("y_lo", [P, 32, T], F32R, stack=mrg)
        att_lo = sb("att_lo", [P, KT, T], F32R, stack=mrg)
        sga = sb("sga", [P, TB, CW], stack=mrg)
        sgb = sb("sgb", [P, TB, CW], stack=mrg)
        y_hi = sb("y_hi", [P, 32, T], F32R, stack=mrg)
        att_hi = sb("att_hi", [P, KT, T], F32R, stack=mrg)
        merged = sb("merged", [P, TB, D], stack=mrg)
        mrg.close()

        mlp = ExitStack()
        h_tm = sb("h_tm", [P, TB, D], stack=mlp)
        u2 = sb("u2", [P, TB, D], stack=mlp)
        relu = sb("relu", [P, 4, T], stack=mlp)
        relu2 = sb("relu2", [P, 4, T], stack=mlp)
        fw = sb("fw", [P, D], stack=mlp)
        hT_hi = sb("hT_hi", [P, 32, T], F32R, stack=mlp)
        hT_lo = sb("hT_lo", [P, 32, T], F32R, stack=mlp)
        mlp.close()

        acc = [ctx.enter_context(nc.psum_tensor(f"acc{n}", [P, 2, 512], F32)) for n in range(2)]
        mp = ctx.enter_context(nc.psum_tensor("mp", [P, 4, 512], F32))

        loaded = [sem(f"loaded{n}") for n in range(RING)]
        hi_ready, lo_ready, unit_used = sem("hi_ready"), sem("lo_ready"), sem("unit_used")
        chunk_free = [sem(f"chunk_free{n}") for n in range(2)]
        x_loaded, small_loaded = sem("x_loaded"), sem("small_loaded")
        table_loaded = sem("table_loaded")
        ss_ready, stat_step, rstd_ready, xn_ready = sem("ss_ready"), sem("stat_step"), sem("rstd_ready"), sem("xn_ready")
        ln_ready, ln_step = sem("ln_ready"), sem("ln_step")
        tr_done, st_hi_done, st_lo_done = sem("tr_done"), sem("st_hi_done"), sem("st_lo_done")
        dt_step, dt_act, dt_ready = sem("dt_step"), sem("dt_act"), sem("dt_ready")
        dtT_done, tmcols_ready, rows_stored = sem("dtT_done"), sem("tmcols_ready"), sem("rows_stored")
        line_done, line_copied, skew_stored = sem("line_done"), sem("line_copied"), sem("skew_stored")
        pads_ready, kv_copied, kv_spread = sem("pads_ready"), sem("kv_copied"), sem("kv_spread")
        q_copied = sem("q_copied")
        xraw_ready, conv_step, conv_done, silu_done = sem("xraw_ready"), sem("conv_step"), sem("conv_done"), sem("silu_done")
        cb_done, cbm_ready = sem("cb_done"), sem("cbm_ready")
        dec_loaded, clamped, dec_exp, mix_ready = sem("dec_loaded"), sem("clamped"), sem("dec_exp"), sem("mix_ready")
        bias_loaded = sem("bias_loaded")
        scores_done, sm_step, shifted, exped = sem("scores_done"), sem("sm_step"), sem("shifted"), sem("exped")
        probs_ready, pT_done, pT_copied = sem("probs_ready"), sem("pT_done"), sem("pT_copied")
        pv_done, att_copied = sem("pv_done"), sem("att_copied")
        xT_done, xdt_ready, y_done, z_ready = sem("xT_done"), sem("xdt_ready"), sem("y_done"), sem("z_ready")
        gate_step, gated, squared, sumsq_done = sem("gate_step"), sem("gated"), sem("squared"), sem("sumsq_done")
        cb_step, fold_step, folded = sem("cb_step"), sem("fold_step"), sem("folded")
        gn_step, ms_ready, gn_ln, rstd0_ready, y_out = sem("gn_step"), sem("ms_ready"), sem("gn_ln"), sem("rstd0_ready"), sem("y_out")
        y_hi_done, y_lo_done, att_lo_done = sem("y_hi_done"), sem("y_lo_done"), sem("att_lo_done")
        qkv_ready, mg_step, mg_done = sem("qkv_ready"), sem("mg_step"), sem("mg_done")
        h_loaded, h_step, fw_loaded = sem("h_loaded"), sem("h_step"), sem("fw_loaded")
        relu_done, relu_sq, hT_hi_done, hT_lo_done = sem("relu_done"), sem("relu_sq"), sem("hT_hi_done"), sem("hT_lo_done")
        out_ready, stored = sem("out_ready"), sem("stored")

        def spread(ap, *dims):
            return bass.AP(ap.tensor, ap.offset, [list(ap.ap[0])] + [list(d) for d in dims])

        block = ctx.enter_context(nc.Block())

        @block.sync
        def _(sp):
            sp.dma_start(x_tm[:, 0, :], x[0:P, :]).then_inc(x_loaded, 16)
            sp.dma_start(x_tm[:, 1, :], x[P:T, :]).then_inc(x_loaded, 16)
            sp.dma_start(cols[:, :], cols_in).then_inc(small_loaded, 16)
            sp.dma_start(consts[:, :], consts_in).then_inc(small_loaded, 16)

            def unit(n, src):
                slot = n.mod(RING)
                if n.c >= RING:
                    sp.wait_ge(lo_ready, (n + (1 - RING)).val())
                sp.dma_start(raw[:, slot, :].rearrange("p (k c) -> p k c", k=src.shape[1]), src).then_inc(loaded[slot], 16)

            def chunk(ch, w, col, row0=0):
                for u in range(ch.units):
                    r = row0 + u * KPU * P
                    rows = w[r:r + KPU * P] if isinstance(r, int) else w[bass.ds(r, KPU * P)]
                    src = rows[:, col:col + CW] if isinstance(col, int) else rows[:, bass.ds(col, CW)]
                    unit(ch.unit + u, src.rearrange("(k p) c -> p k c", p=P))

            for u in range(DT_UNITS):
                unit(Lin(u), w_in[u * (D // 2):(u + 1) * (D // 2), DT_OFF:DT_OFF + P].rearrange("(k p) c -> p k c", p=P))
            chunk(K_CHUNK, w_in, K_OFF)
            chunk(V_CHUNK, w_in, V_OFF)
            for j in range(4):
                chunk(bc_chunk(j), w_in, XBC_OFF + DI + j * CW)
            for j in range(4):
                chunk(q_chunk(j), w_in, Q_OFF + j * CW)
            chunk(x_chunk(0), w_in, XBC_OFF)
            chunk(z_chunk(0), w_in, Z_OFF)
            with sp.Fori(0, SSM_G - 1) as g:
                chunk(next_x(g), w_in, g * CW + (XBC_OFF + CW))
                chunk(next_z(g), w_in, g * CW + (Z_OFF + CW))
            chunk(ga_chunk(0), w_in, GA_OFF)
            chunk(gb_chunk(0), w_in, GB_OFF)
            with sp.Fori(0, 3) as j:
                chunk(ssm_chunk(j), w_ssm, j * CW)
                chunk(att_chunk(j), w_att, j * CW)
                chunk(next_ga(j), w_in, j * CW + (GA_OFF + CW))
                chunk(next_gb(j), w_in, j * CW + (GB_OFF + CW))
            chunk(ssm_chunk(3), w_ssm, 3 * CW)
            chunk(att_chunk(3), w_att, 3 * CW)
            for j in range(4):
                chunk(out_chunk(j), w_out, j * CW)
            with sp.Fori(0, 2) as half:
                with sp.Fori(0, 4) as pair:
                    for j in range(2):
                        chunk(up_chunk(half, j, pair), w_up, half * (8 * CW) + (pair * (2 * CW) + j * CW))
                for j in range(4):
                    chunk(down_chunk(half, j), w_down, j * CW, half * (DFF // 2))
            for b in range(TB):
                sp.wait_ge(out_ready, b + 1)
                sp.dma_start(out[b * P:(b + 1) * P, :], u2[:, b, :]).then_inc(stored, 16)
            sp.wait_ge(stored, 16 * TB)

        @block.gpsimd
        def _(pool):
            pool.memset(kdup[:, :, 0:L], 0.0).then_inc(pads_ready, 1)
            pool.memset(v_win[0:L, 0, :], 0.0).then_inc(pads_ready, 1)
            pool.memset(xraw[:, :, 0:3], 0.0).then_inc(pads_ready, 1)

            def group_qkv(g):
                pool.tensor_copy(q_g[:, :, :], qatt[:, cut_at(g, 2), :]).then_inc(qkv_ready, 1)
                pool.tensor_copy(k_g[:, :], kdup[:, cut_at(g, 1), :].rearrange("p a t -> p (a t)")).then_inc(qkv_ready, 1)
                pool.tensor_copy(v_g[:, :, :], v_win[:, :, cut_at(g, HD)]).then_inc(qkv_ready, 1)

            def group(g):
                it = at(0, 1, g)
                pool.wait_ge(dec_exp, (it.times(2) + 2).val())
                pool.tensor_copy(cb_g[:, :], cbm[:, cut_at(g, 1), :].rearrange("p a t -> p (a t)")).then_inc(cb_step, 1)
                pool.wait_ge(cb_step, (it + 1).val())
                for k in range(2):
                    pool.tensor_tensor(dec[k][:, :, :], dec[k][:, :, :], spread(cb_g[:, :], (0, 4), (1, SW)), ALU.mult).then_inc(mix_ready, 1)
                pool.wait_ge(squared, (it + 1).val())
                pool.tensor_tensor(sq[:, 0:2, :], sq[:, 0:2, :], sq[:, 2:4, :], ALU.add).then_inc(fold_step, 1)
                pool.wait_ge(fold_step, (it + 1).val())
                pool.tensor_tensor(sq[:, 0, :], sq[:, 0, :], sq[:, 1, :], ALU.add).then_inc(folded, 1)

            pool.wait_ge(chunk_free[1], q_chunk(3).left.val())
            pool.wait_ge(cbm_ready, SSM_G)
            pool.wait_ge(kv_spread, 64)
            group_qkv(0)
            with pool.Fori(0, SSM_G - 1) as g:
                group(g)
                pool.wait_ge(pv_done, g + 1)
                group_qkv(g + 1)
            group(SSM_G - 1)

            for p in range(4):
                pool.wait_ge(y_hi_done, 8 + p + 1)
                s = cut_at(p, 4)
                pool.tensor_tensor(att_lo[:, s, :], qatt[:, s, :], att_hi[:, s, :], ALU.subtract).then_inc(att_lo_done, 1)

        @block.scalar
        def _(act):
            def cut(n, count, hooks=None):
                for u in range(count):
                    for hook in (hooks or {}).get(u, ()):
                        hook()
                    m = n + u
                    slot = m.mod(RING)
                    act.wait_ge(loaded[slot], (m.over(RING) + 1).times(16).val())
                    if m.c >= RING:
                        act.wait_ge(unit_used, (m + (1 - RING)).val())
                    act.activation(w_hi[:, slot, :], raw[:, slot, :], ACT.Copy).then_inc(hi_ready, 1)

            def wait_full(ch):
                act.wait_ge(unit_used, ch.end.val())

            def cut_chunk(ch, hooks=None):
                cut(ch.unit, ch.units, hooks)

            def statistics(r, src):
                for b in range(TB):
                    act.activation(u2_like(r)[:, b, :], src[:, b, :], ACT.Square,
                                   accum_out=stat[:, b:b + 1]).then_inc(ss_ready, 1)
                act.wait_ge(stat_step, 4 * r + 1)
                act.activation(stat[:, 4:6], stat[:, 2:4], ACT.Ln).then_inc(ln_step, 1)
                act.wait_ge(ln_step, r + 1)
                act.activation(stat[:, 6:8], stat[:, 4:6], ACT.Exp, scale=-0.5).then_inc(ln_ready, 1)

            def u2_like(r):
                return (y32[:, 16:32, :].rearrange("p (b j) t -> p b (j t)", b=TB), u2, u2)[r]

            def stationary(r, wcol):
                for kp in range(KT // 2):
                    act.wait_ge(tr_done, 8 * r + kp + 1)
                    for j in range(2):
                        k = 2 * kp + j
                        src = mp[:, kp % 4, j * T:(j + 1) * T]
                        scale = 1.0 if wcol is None else cols[:, wcol + k:wcol + k + 1]
                        ins = act.activation(st_hi[:, k, :], src, ACT.Copy, scale=scale)
                        ins.then_inc(st_hi_done, 1)

            act.wait_ge(x_loaded, 32)
            statistics(0, x_tm)
            act.wait_ge(small_loaded, 32)
            act.dma_start(relt_sb, rel_table).then_inc(table_loaded, 16)
            act.dma_start(onehot_sb, onehot_in).then_inc(table_loaded, 16)
            stationary(0, C_N1)
            cut(Lin(0), DT_UNITS)

            def bias_line():
                act.wait_ge(line_done, 1)
                act.activation(line_sb, mp[0:ATT_H, 3, 0:LINE], ACT.Copy).then_inc(line_copied, 1)
                act.wait_ge(line_copied, 1)
                src = bass.AP(line_sb.tensor, line_sb.offset, [list(line_sb.ap[0]), [0, L], [1, LINE]])
                act.dma_start(bias_skew, src).then_inc(skew_stored, 16)

            def dt_bias():
                act.wait_ge(unit_used, DT_UNITS)
                act.activation(dtw[:, 0, :], mp[0:SSM_H, 0, 0:T], ACT.Identity,
                               bias=cols[0:SSM_H, C_DTB:C_DTB + 1]).then_inc(dt_act, 1)
                act.activation(smx[0:SSM_H, 0, 0:1], cols[0:SSM_H, C_ALOG:C_ALOG + 1], ACT.Exp).then_inc(dt_act, 1)

            def dt_exp():
                act.wait_ge(dt_step, 2)
                act.activation(dtw[:, 2, :], dtw[:, 1, :], ACT.Exp).then_inc(dt_act, 1)

            def dt_ln():
                act.wait_ge(dt_step, 3)
                act.activation(dtw[:, 4, :], dtw[:, 3, :], ACT.Ln).then_inc(dt_act, 1)

            def store_rows():
                act.wait_ge(dt_ready, 1)
                rows = dtw[:, 10:13, :].rearrange("h a t -> h (a t)")
                for half in range(2):
                    act.dma_start(decay_rows[half], rows[:, half * SW:(half + 1) * SW]).then_inc(rows_stored, 16)

            def load_decays(g):
                for n in range(2):
                    for half in range(2):
                        first = g * HPG + 4 * n
                        src = decay_rows[half, first:first + 4] if isinstance(first, int) else decay_rows[half, bass.ds(first, 4)]
                        src = bass.AP(src.tensor, src.offset, [[0, L], [SW, 4], [1, SW]])
                        act.dma_start(dec[n][half * L:(half + 1) * L, :, :], src).then_inc(dec_loaded, 16)

            def load_bias(g):
                for half in range(2):
                    src = bias_skew[g * 4:g * 4 + 4] if isinstance(g, int) else bias_skew[bass.ds(g * 4, 4)]
                    src = bass.AP(src.tensor, src.offset + (L - 1), [[LINE - 1, L], [L * LINE, 4], [1, WIN]])
                    act.dma_start(bias_g[half * L:(half + 1) * L, :, :], src).then_inc(bias_loaded, 16)

            def banks(ch):
                return acc[ch.bank][:, :, :].rearrange("p b (j t) -> p (b j) t", t=T)

            def keys_out():
                wait_full(K_CHUNK)
                act.wait_ge(pads_ready, 3)
                a = banks(K_CHUNK)
                act.activation(kdup[0:L, 0:KV:2, L:L + T], a[0:L], ACT.Copy).then_inc(kv_copied, 1)
                act.activation(kdup[L:P, 1:KV:2, L:L + T], a[L:P], ACT.Copy).then_inc(chunk_free[0], 1)
                act.wait_ge(kv_copied, 1)
                act.wait_ge(chunk_free[0], K_CHUNK.left.val())
                act.dma_start(kdup[L:P, 0:KV:2, L:L + T], kdup[0:L, 0:KV:2, L:L + T]).then_inc(kv_spread, 16)
                act.dma_start(kdup[0:L, 1:KV:2, L:L + T], kdup[L:P, 1:KV:2, L:L + T]).then_inc(kv_spread, 16)

            def values_out():
                wait_full(V_CHUNK)
                act.activation(v_win[:, 1:NCH:2, :], acc[1][:, :, :], ACT.Copy).then_inc(chunk_free[1], 1)
                act.wait_ge(chunk_free[1], V_CHUNK.left.val())
                act.dma_start(v_win[L:P, 0:NCH:2, :], v_win[0:L, 1:NCH:2, :]).then_inc(kv_spread, 16)
                act.dma_start(v_win[0:L, 2, :], v_win[L:P, 1, :]).then_inc(kv_spread, 16)

            def queries_out(j):
                ch = q_chunk(j)
                wait_full(ch)
                act.activation(qatt[:, 4 * j:4 * j + 4, :], banks(ch), ACT.Copy, scale=HD ** -0.5).then_inc(chunk_free[ch.bank], 1)

            def conv_in(ch):
                wait_full(ch)
                act.activation(xraw[:, :, 3:3 + T], banks(ch), ACT.Copy).then_inc(chunk_free[ch.bank], 1)

            def conv_silu(k, dst):
                act.wait_ge(conv_done, (k + 1).val())
                act.activation(dst, xc[:, :, :], ACT.Silu).then_inc(silu_done, 1)

            cut_chunk(K_CHUNK, {4: [bias_line, dt_bias], 6: [dt_exp]})
            cut_chunk(V_CHUNK, {1: [dt_ln], 3: [keys_out], 5: [store_rows]})
            cut_chunk(bc_chunk(0), {3: [values_out]})
            for j in range(1, 4):
                cut_chunk(bc_chunk(j), {3: [lambda: conv_in(bc_chunk(j - 1))],
                                        6: [lambda: conv_silu(Lin(j - 1), bc[:, 4 * (j - 1):4 * j, :])]})
            cut_chunk(q_chunk(0), {3: [lambda: conv_in(bc_chunk(3))], 6: [lambda: conv_silu(Lin(3), bc[:, 12:16, :])]})
            for j in range(1, 4):
                cut_chunk(q_chunk(j), {3: [lambda: queries_out(j - 1)]})

            def first_loads():
                act.wait_ge(rows_stored, 32)
                load_decays(0)
                act.wait_ge(skew_stored, 16)
                load_bias(0)

            cut_chunk(x_chunk(0), {3: [lambda: queries_out(3)], 4: [first_loads]})

            def group(g):
                it = at(0, 1, g)
                z = z_chunk(g)

                def decay_clamp(k):
                    act.wait_ge(dec_loaded, at(64, 64, g).val())
                    for h in range(4):
                        for blk in range(TB):
                            s = tmcols[:, 2 + blk, cut_at(g * HPG + (4 * k + h), 1)]
                            lo, hi = (0, T) if blk == 0 else (T, SW)
                            ins = act.activation(dec[k][:, h, lo:hi], dec[k][:, h, lo:hi], ACT.Relu, bias=s, scale=-1.0)
                    ins.then_inc(clamped, 1)

                def decay_exp(k):
                    act.wait_ge(clamped, (it.times(2) + (k + 1)).val())
                    act.activation(dec[k][:, :, :], dec[k][:, :, :], ACT.Exp, scale=-1.0).then_inc(dec_exp, 1)

                def softmax_exp():
                    act.wait_ge(shifted, (it.times(2) + 2).val())
                    act.activation(smx[:, 1, :], smx[:, 1, :], ACT.Exp).then_inc(exped, 1)
                    act.activation(probs[:, :, :], probs[:, :, :], ACT.Exp).then_inc(exped, 1)

                def probsT_out():
                    act.wait_ge(pT_done, (it + 1).val())
                    act.activation(probsT[:, :, :], mp[:, 0:2, :], ACT.Copy).then_inc(pT_copied, 1)

                def z_silu():
                    wait_full(z)
                    act.activation(zs[:, :, :], banks(z), ACT.Silu).then_inc(chunk_free[1], 1)

                def square():
                    act.wait_ge(gated, (it + 1).val())
                    act.activation(sq, y32[:, cut_at(g, 4), :], ACT.Square).then_inc(squared, 1)

                def att_out():
                    act.wait_ge(pv_done, (it + 1).val())
                    act.activation(qatt[:, cut_at(g, 2), :], mp[:, 0, :].rearrange("p (j t) -> p j t", j=2),
                                   ACT.Copy).then_inc(att_copied, 1)

                def group_rstd():
                    act.wait_ge(ms_ready, (it + 1).val())
                    act.activation(rstd_g, ms_g, ACT.Ln).then_inc(gn_ln, 1)
                    act.wait_ge(gn_ln, (it + 1).val())
                    act.activation(rstd_g, rstd_g, ACT.Exp, scale=-0.5).then_inc(rstd0_ready, 1)

                def next_bias():
                    act.wait_ge(shifted, (it.times(2) + 2).val())
                    load_bias(g + 1)

                def next_decays():
                    act.wait_ge(y_done, (it + 1).val())
                    load_decays(g + 1)

                steps = {0: [lambda: decay_clamp(0)], 1: [lambda: decay_clamp(1)], 3: [lambda: conv_in(x_chunk(g))],
                         4: [lambda: decay_exp(0)], 5: [lambda: decay_exp(1)],
                         6: [lambda: conv_silu(it + 4, x_fm[:, :, :])], 11: [softmax_exp],
                         12: [z_silu], 15: [probsT_out, square], 17: [att_out], 18: [group_rstd]}
                if not is_last(g):
                    steps[13] = [next_bias, next_decays]
                return steps

            cut_chunk(z_chunk(0), part(group(0), 0))
            with act.Fori(0, SSM_G - 1) as g:
                cut_chunk(next_x(g), part(group(g), UPC))
                cut_chunk(next_z(g), joined(part(group(g), 2 * UPC), part(group(g + 1), 0)))
            cut_chunk(ga_chunk(0), part(group(SSM_G - 1), UPC))

            def gate(ch, dst):
                wait_full(ch)
                act.activation(dst, acc[ch.bank][:, :, :], ACT.Sigmoid).then_inc(chunk_free[ch.bank], 1)

            def cut_y(part):
                if part == 0:
                    act.wait_ge(y_out, 4 * (SSM_G - 1))
                    act.wait_ge(gated, SSM_G)
                if part == 7:
                    act.wait_ge(y_out, 4 * SSM_G)
                if part < 8:
                    dst, src = y_hi[:, cut_at(part, 4), :], y32[:, cut_at(part, 4), :]
                else:
                    dst, src = att_hi[:, cut_at(part - 8, 4), :], qatt[:, cut_at(part - 8, 4), :]
                act.activation(dst, src, ACT.Copy).then_inc(y_hi_done, 1)

            cut_chunk(gb_chunk(0), joined(part(group(SSM_G - 1), 2 * UPC), {
                3: [lambda: gate(ga_chunk(0), sga[:, :, :])],
                4: [lambda: cut_y(0), lambda: cut_y(1)], 5: [lambda: cut_y(2), lambda: cut_y(3)],
                6: [lambda: cut_y(4), lambda: cut_y(5)], 7: [lambda: cut_y(6)]}))
            for p in range(7, 12):
                cut_y(p)

            def merge_gates(j, last):
                cut_chunk(ssm_chunk(j), {3: [lambda: gate(gb_chunk(j), sgb[:, :, :])]})
                cut_chunk(att_chunk(j))
                if not last:
                    cut_chunk(next_ga(j))

                    def gate_a():
                        act.wait_ge(chunk_free[0], ssm_chunk(j).left.val())
                        gate(next_ga(j), sga[:, :, :])

                    def sgb_used():
                        act.wait_ge(mg_done, at(2, 2, j).val())
                    cut_chunk(next_gb(j), {3: [gate_a], 7: [sgb_used]})

            with act.Fori(0, 3) as j:
                merge_gates(j, False)
            merge_gates(3, True)

            cut(out_chunk(0).unit, RING)
            act.wait_ge(mg_done, 8)
            for b in range(TB):
                act.dma_start(h_tm[:, b, :], x[b * P:(b + 1) * P, :]).then_inc(h_loaded, 16)
            act.dma_start(fw[:, :], fnorm.partition_broadcast(P)).then_inc(fw_loaded, 16)
            stationary(1, None)
            cut(out_chunk(0).unit + RING, UPC - RING)
            for j in range(1, 4):
                cut_chunk(out_chunk(j))
            act.wait_ge(chunk_free[1], out_chunk(3).left.val())
            statistics(1, h_tm)
            stationary(2, C_N2)

            def up_hooks(half, j, pair=None):
                ch = up_chunk(half, j, pair)
                q = Lin(j).along(8, half)
                tiles = cut_at(j, 4)
                if pair is not None:
                    q = q.along(2, pair)
                    tiles = bass.ds(pair * 8 + 4 * j, 4)

                def relu_():
                    wait_full(ch)
                    act.activation(relu[:, :, :], banks(ch), ACT.Relu).then_inc(chunk_free[ch.bank], 1)
                    act.wait_ge(chunk_free[ch.bank], ch.left.val())

                def square_():
                    act.activation(relu2[:, :, :], relu[:, :, :], ACT.Square).then_inc(relu_sq, 1)
                    act.wait_ge(relu_sq, (q + 1).val())

                def hi_():
                    act.activation(hT_hi[:, tiles, :], relu2[:, :, :], ACT.Copy).then_inc(hT_hi_done, 1)

                def lo_done():
                    act.wait_ge(hT_lo_done, (q + 1).val())
                return {3: [relu_], 4: [square_], 5: [hi_], 7: [lo_done]}

            with act.Fori(0, 2) as half:
                cut_chunk(up_chunk(half, 0))
                with act.Fori(0, 3) as pair:
                    cut_chunk(up_chunk(half, 1, pair), up_hooks(half, 0, pair))
                    cut_chunk(up_chunk(half, 2, pair), up_hooks(half, 1, pair))
                cut_chunk(up_chunk(half, 7), up_hooks(half, 6))
                cut_chunk(down_chunk(half, 0), up_hooks(half, 7))
                for j in range(1, 4):
                    cut_chunk(down_chunk(half, j))
            act.wait_ge(chunk_free[1], N_MLP // 2 + HALF_N)
            statistics(2, h_tm)

        @block.vector
        def _(dve):
            def cut(n, count, hooks=None):
                for u in range(count):
                    for hook in (hooks or {}).get(u, ()):
                        hook()
                    m = n + u
                    slot = m.mod(RING)
                    dve.wait_ge(hi_ready, (m + 1).val())
                    dve.tensor_tensor(w_lo[:, slot, :], raw[:, slot, :], w_hi[:, slot, :], ALU.subtract).then_inc(lo_ready, 1)

            def wait_full(ch):
                dve.wait_ge(unit_used, ch.end.val())

            def cut_chunk(ch, hooks=None):
                cut(ch.unit, ch.units, hooks)

            def statistics(r, src, dst):
                dve.wait_ge(ss_ready, 2 * (r + 1))
                dve.tensor_scalar(stat[:, 2:4], stat[:, 0:2], 1.0 / D, EPS, ALU.mult, ALU.add).then_inc(stat_step, 1)
                dve.wait_ge(ln_ready, r + 1)
                y0, ms, t = stat[:, 6:8], stat[:, 2:4], stat[:, 8:10]
                dve.tensor_tensor(t, y0, y0, ALU.mult).then_inc(stat_step, 1)
                dve.wait_ge(stat_step, 4 * r + 2)
                dve.tensor_tensor(t, t, ms, ALU.mult).then_inc(stat_step, 1)
                dve.wait_ge(stat_step, 4 * r + 3)
                dve.tensor_scalar(t, t, -0.5, 1.5, ALU.mult, ALU.add).then_inc(stat_step, 1)
                dve.wait_ge(stat_step, 4 * r + 4)
                dve.tensor_tensor(stat[:, 10:12], y0, t, ALU.mult).then_inc(rstd_ready, 1)
                dve.wait_ge(rstd_ready, r + 1)
                if dst is not None:
                    for b in range(TB):
                        dve.tensor_scalar(dst[:, b, :], src[:, b, :], stat[:, 10 + b:11 + b], None, ALU.mult).then_inc(xn_ready, 1)

            def stationary(r, wcol):
                for kp in range(KT // 2):
                    for j in range(2):
                        k = 2 * kp + j
                        src = mp[:, kp % 4, j * T:(j + 1) * T]
                        dve.wait_ge(st_hi_done, KT * r + 2 * kp + 2)
                        scale = 1.0 if wcol is None else cols[:, wcol + k:wcol + k + 1]
                        dve.scalar_tensor_tensor(st_lo[:, k, :], src, scale, st_hi[:, k, :],
                                                 ALU.mult, ALU.subtract).then_inc(st_lo_done, 1)

            statistics(0, x_tm, x_tm)
            dve.wait_ge(small_loaded, 32)
            stationary(0, C_N1)
            cut(Lin(0), DT_UNITS)

            def step(ins, s, count):
                ins.then_inc(s, 1)
                dve.wait_ge(s, count)

            def dt_a():
                dve.wait_ge(dt_act, 2)
                v = dtw[:, 0, :]
                step(dve.tensor_scalar(dtw[:, 1, :], v, -1.0, None, ALU.mult), dt_step, 1)
                step(dve.tensor_tensor(dtw[:, 1, :], v, dtw[:, 1, :], ALU.min), dt_step, 2)

            def dt_b():
                dve.wait_ge(dt_act, 3)
                step(dve.tensor_scalar(dtw[:, 3, :], dtw[:, 2, :], 1.0, None, ALU.add), dt_step, 3)

            def dt_c():
                step(dve.tensor_scalar(dtw[:, 5, :], dtw[:, 3, :], -1.0, None, ALU.add), dt_step, 4)
                step(dve.tensor_scalar(dtw[:, 6, :], dtw[:, 5, :], 0.0, None, ALU.is_equal), dt_step, 5)
                step(dve.tensor_tensor(dtw[:, 5, :], dtw[:, 5, :], dtw[:, 6, :], ALU.add), dt_step, 6)
                step(dve.reciprocal(dtw[:, 5, :], dtw[:, 5, :]), dt_step, 7)
                dve.wait_ge(dt_act, 4)
                step(dve.tensor_tensor(dtw[:, 6, :], dtw[:, 6, :], dtw[:, 4, :], ALU.add), dt_step, 8)
                step(dve.tensor_tensor(dtw[:, 6, :], dtw[:, 6, :], dtw[:, 5, :], ALU.mult), dt_step, 9)
                step(dve.tensor_tensor(dtw[:, 6, :], dtw[:, 6, :], dtw[:, 2, :], ALU.mult), dt_step, 10)
                step(dve.scalar_tensor_tensor(dtw[:, 8, :], dtw[:, 0, :], 0.0, dtw[:, 6, :], ALU.max, ALU.add), dt_step, 11)
                step(dve.tensor_scalar(dtw[:, 9, :], dtw[:, 8, :], smx[0:SSM_H, 0, 0:1], -1.0, ALU.mult, ALU.mult), dt_step, 12)

            def cumulate():
                n = 12
                src, dst = 9, 7
                for s in (1, 2, 4, 8, 16, 32):
                    a = dtw[:, src, :].rearrange("h (c l) -> h c l", l=L)
                    b = dtw[:, dst, :].rearrange("h (c l) -> h c l", l=L)
                    dve.tensor_tensor(b[:, :, s:], a[:, :, s:], a[:, :, :L - s], ALU.add).then_inc(dt_step, 1)
                    n += 2
                    step(dve.tensor_copy(b[:, :, :s], a[:, :, :s]), dt_step, n)
                    src, dst = dst, src
                assert src == 9
                acs = dtw[:, 9, :].rearrange("h (c l) -> h c l", l=L)
                tot = [acs[:, c, L - 1:L] for c in range(NCH)]
                s01, s12, s012 = smx[0:SSM_H, 2, 0:1], smx[0:SSM_H, 2, 1:2], smx[0:SSM_H, 2, 2:3]
                dve.tensor_tensor(s01, tot[0], tot[1], ALU.add).then_inc(dt_step, 1)
                dve.tensor_tensor(s12, tot[1], tot[2], ALU.add).then_inc(dt_step, 1)
                n += 2
                dve.wait_ge(dt_step, n)
                step(dve.tensor_tensor(s012, s01, tot[2], ALU.add), dt_step, n + 1)
                n += 1
                rows = dtw[:, 10:13, :].rearrange("h a t -> h (a t)")
                lower, upper = rows[:, 0:SW].rearrange("h (c l) -> h c l", l=L), rows[:, SW:2 * SW].rearrange("h (c l) -> h c l", l=L)

                def put(dst, c, add, last=False):
                    if c is None:
                        ins = dve.memset(dst, 0.0)
                    elif add is None:
                        ins = dve.tensor_copy(dst, acs[:, c, :])
                    else:
                        ins = dve.tensor_scalar(dst, acs[:, c, :], add, None, ALU.add)
                    ins.then_inc(dt_ready if last else dt_step, 1)
                for k, (c, add) in enumerate([(0, None), (1, tot[0]), (2, s01), (3, s012), (2, None), (3, tot[2])]):
                    put(lower[:, k, :], c, add)
                for k, (c, add) in enumerate([(None, None), (1, None), (2, tot[1]), (3, s12), (None, None), (3, None)]):
                    put(upper[:, k, :], c, add, last=(k == 5))

            def dt_columns():
                dve.wait_ge(dtT_done, 1)
                dve.tensor_copy(tmcols[:, :, :], mp[:, 2, 0:4 * SSM_H].rearrange("p (a h) -> p a h", a=4)).then_inc(tmcols_ready, 1)

            cut_chunk(K_CHUNK, {5: [dt_a], 7: [dt_b]})
            cut_chunk(V_CHUNK, {2: [dt_c], 4: [cumulate]})
            cut_chunk(bc_chunk(0), {6: [dt_columns]})

            def conv(k, tile0, ch):
                def half(t0):
                    def run():
                        if t0 == 0:
                            dve.wait_ge(chunk_free[ch.bank], ch.left.val())
                        base = k.times(15) + (4 * t0)
                        for tap in range(4):
                            for t in (t0, t0 + 1):
                                src = xraw[:, t, tap:tap + T]
                                wt = tile0 * 4 + (4 * t + C_CONVW + tap)
                                wcol = cols[:, cut_at(wt, 1)]
                                if tap == 0:
                                    ins = dve.tensor_scalar(xc[:, t, :], src, wcol, cols[:, cut_at(tile0 + (t + C_CONVB), 1)],
                                                            ALU.mult, ALU.add)
                                else:
                                    dve.wait_ge(conv_step, (base + (2 * (tap - 1) + (t - t0) + 1)).val())
                                    ins = dve.scalar_tensor_tensor(xc[:, t, :], src, wcol, xc[:, t, :], ALU.mult, ALU.add)
                                ins.then_inc(conv_done if (tap, t) == (3, 3) else conv_step, 1)
                    return run
                return [half(0)], [half(2)]

            for j in range(1, 4):
                a, b = conv(Lin(j - 1), DI // P + 4 * (j - 1), bc_chunk(j - 1))
                cut_chunk(bc_chunk(j), {4: a, 5: b})
            a, b = conv(Lin(3), DI // P + 12, bc_chunk(3))
            cut_chunk(q_chunk(0), {4: a, 5: b})

            def mask_cb(g):
                dve.wait_ge(cb_done, g + 1)
                dve.tensor_tensor(cbm[:, g, :], mp[:, g % 4, 0:SW], mask, ALU.mult).then_inc(cbm_ready, 1)

            cut_chunk(q_chunk(1), {5: [lambda: mask_cb(0), lambda: mask_cb(1)], 6: [lambda: mask_cb(2), lambda: mask_cb(3)]})
            cut_chunk(q_chunk(2), {3: [lambda: mask_cb(4), lambda: mask_cb(5)], 4: [lambda: mask_cb(6), lambda: mask_cb(7)]})
            cut_chunk(q_chunk(3))
            cut_chunk(x_chunk(0))

            def group(g):
                it = at(0, 1, g)
                z = z_chunk(g)
                sm = it.times(7)
                pr = probs[:, :, :].rearrange("p b (h k) -> p (b h) k", k=WIN)
                mx, less, den, rec = (smx[:, n, :] for n in range(4))
                sk = spread(cols[:, cut_at_off(g, 4, C_SINK)], (1, 2), (0, TB), (2, 2))
                mx2 = mx.rearrange("p (e b t) -> p e b t", e=2, b=TB)

                def softmax_max():
                    dve.wait_ge(scores_done, (it + 1).val())
                    dve.wait_ge(bias_loaded, at(32, 32, g).val())
                    for e in range(2):
                        be = spread(bias_g[:, e, :], (0, TB), (2 * WIN, 2), (1, WIN))
                        ins = dve.tensor_tensor(probs[:, e, :].rearrange("p (b t k) -> p b t k", b=TB, t=2),
                                                mp[:, e, :].rearrange("p (b t k) -> p b t k", b=TB, t=2), be, ALU.add)
                    ins.then_inc(sm_step, 1)
                    dve.wait_ge(sm_step, (sm + 1).val())
                    dve.memset(probs[0:L, :, 0:2 * WIN].rearrange("p e (t k) -> p e t k", t=2)[:, :, :, 0:L], MASKED).then_inc(sm_step, 1)
                    dve.wait_ge(sm_step, (sm + 2).val())
                    dve.tensor_reduce(mx, pr, AX.X, ALU.max).then_inc(sm_step, 1)
                    dve.wait_ge(sm_step, (sm + 3).val())
                    dve.tensor_tensor(mx2, mx2, sk, ALU.max).then_inc(sm_step, 1)

                def softmax_shift():
                    dve.wait_ge(sm_step, (sm + 4).val())
                    dve.tensor_tensor(less.rearrange("p (e b t) -> p e b t", e=2, b=TB), sk, mx2, ALU.subtract).then_inc(shifted, 1)
                    dve.tensor_tensor(pr, pr, spread(mx, (1, 8), (0, WIN)), ALU.subtract).then_inc(shifted, 1)

                def softmax_sum():
                    dve.wait_ge(exped, (it.times(2) + 2).val())
                    dve.tensor_reduce(den, pr, AX.X, ALU.add).then_inc(sm_step, 1)
                    dve.wait_ge(sm_step, (sm + 5).val())
                    dve.tensor_tensor(den, den, less, ALU.add).then_inc(sm_step, 1)
                    dve.wait_ge(sm_step, (sm + 6).val())
                    dve.reciprocal(rec, den).then_inc(sm_step, 1)

                def softmax_scale():
                    dve.wait_ge(sm_step, (sm + 7).val())
                    dve.tensor_tensor(pr, pr, spread(rec, (1, 8), (0, WIN)), ALU.mult).then_inc(probs_ready, 1)

                def times_dt():
                    dve.wait_ge(xT_done, (it + 1).val())
                    for blk in range(TB):
                        dts = spread(tmcols[:, blk, cut_at(g, HPG)], (1, HPG), (0, HD))
                        dve.tensor_tensor(xdt[:, blk, :].rearrange("p (h d) -> p h d", d=HD),
                                          mp[:, 2 + blk, :].rearrange("p (h d) -> p h d", d=HD), dts, ALU.mult).then_inc(xdt_ready, 1)

                yg = y32[:, cut_at(g, 4), :]

                def add_skip():
                    dve.wait_ge(y_done, (it + 1).val())
                    dve.wait_ge(silu_done, (it + 5).val())
                    for t in range(4):
                        src = mp[:, 2 + t // 2, (t % 2) * T:(t % 2 + 1) * T]
                        dve.scalar_tensor_tensor(yg[:, t, :], x_fm[:, t, :], cols[:, cut_at(g * 4 + (C_SKIP + t), 1)], src,
                                                 ALU.mult, ALU.add).then_inc(gate_step, 1)

                def gate():
                    dve.wait_ge(chunk_free[1], z.left.val())
                    dve.wait_ge(gate_step, at(4, 4, g).val())
                    dve.tensor_tensor(yg, yg, zs[:, :, :], ALU.mult).then_inc(gated, 1)

                def mean_square():
                    dve.wait_ge(sumsq_done, (it + 1).val())
                    dve.tensor_scalar(ms_g, mp[:, 1, 0:T], 1.0 / (4 * P), EPS, ALU.mult, ALU.add).then_inc(ms_ready, 1)

                def normalise():
                    gn = it.times(4)
                    y0, ms, t_ = rstd_g, ms_g, sq[:, 0, :]
                    dve.wait_ge(rstd0_ready, (it + 1).val())
                    dve.tensor_tensor(t_, y0, y0, ALU.mult).then_inc(gn_step, 1)
                    dve.wait_ge(gn_step, (gn + 1).val())
                    dve.tensor_tensor(t_, t_, ms, ALU.mult).then_inc(gn_step, 1)
                    dve.wait_ge(gn_step, (gn + 2).val())
                    dve.tensor_scalar(t_, t_, -0.5, 1.5, ALU.mult, ALU.add).then_inc(gn_step, 1)
                    dve.wait_ge(gn_step, (gn + 3).val())
                    dve.tensor_tensor(t_, y0, t_, ALU.mult).then_inc(gn_step, 1)
                    dve.wait_ge(gn_step, (gn + 4).val())
                    for t in range(4):
                        dve.scalar_tensor_tensor(yg[:, t, :], yg[:, t, :], cols[:, cut_at(g * 4 + (C_SSMN + t), 1)], t_,
                                                 ALU.mult, ALU.mult).then_inc(y_out, 1)

                def scales_read():
                    dve.wait_ge(y_out, at(4, 4, g).val())

                a, b = conv(it + 4, g * 4, x_chunk(g))
                return {4: a, 5: b, 8: [times_dt], 9: [softmax_max], 10: [softmax_shift], 12: [softmax_sum],
                        13: [softmax_scale, add_skip], 14: [gate], 18: [mean_square], 22: [normalise],
                        23: [scales_read]}

            cut_chunk(z_chunk(0), part(group(0), 0))
            with dve.Fori(0, SSM_G - 1) as g:
                cut_chunk(next_x(g), part(group(g), UPC))
                cut_chunk(next_z(g), joined(part(group(g), 2 * UPC), part(group(g + 1), 0)))
            cut_chunk(ga_chunk(0), part(group(SSM_G - 1), UPC))

            def cut_y(p):
                dve.wait_ge(y_hi_done, p + 1)
                s = cut_at(p, 4)
                dve.tensor_tensor(y_lo[:, s, :], y32[:, s, :], y_hi[:, s, :], ALU.subtract).then_inc(y_lo_done, 1)

            cut_chunk(gb_chunk(0), joined(part(group(SSM_G - 1), 2 * UPC), {
                5: [lambda: cut_y(0), lambda: cut_y(1)], 6: [lambda: cut_y(2), lambda: cut_y(3)],
                7: [lambda: cut_y(4), lambda: cut_y(5)]}))
            cut_y(6)
            cut_y(7)

            def merge(j, last):
                ssm, att = ssm_chunk(j), att_chunk(j)

                def mcols(b):
                    return merged[:, b, cut_at(j, CW)]

                def ssm_part():
                    wait_full(ssm)
                    dve.wait_ge(chunk_free[0], ssm.turn.val())
                    for b in range(TB):
                        dve.tensor_tensor(mcols(b), acc[0][:, b, :], sga[:, b, :], ALU.mult).then_inc(mg_step if b == 0 else chunk_free[0], 1)

                def att_part():
                    wait_full(att)
                    dve.wait_ge(chunk_free[1], att.turn.val())
                    for b in range(TB):
                        dve.tensor_tensor(sgb[:, b, :], acc[1][:, b, :], sgb[:, b, :], ALU.mult).then_inc(mg_step if b == 0 else chunk_free[1], 1)
                    dve.wait_ge(chunk_free[0], ssm.left.val())
                    dve.wait_ge(chunk_free[1], att.left.val())
                    for b in range(TB):
                        dve.tensor_tensor(mcols(b), mcols(b), sgb[:, b, :], ALU.add).then_inc(mg_done, 1)
                cut_chunk(ssm)
                cut_chunk(att, {3: [ssm_part]})
                if not last:
                    cut_chunk(next_ga(j), {3: [att_part]})
                    cut_chunk(next_gb(j))
                else:
                    cut(out_chunk(0).unit, RING - 1)
                    att_part()
                    cut(out_chunk(0).unit + (RING - 1), 1)

            with dve.Fori(0, 3) as j:
                merge(j, False)
            merge(3, True)
            stationary(1, None)

            def add_to_h(ch, j):
                wait_full(ch)
                for b in range(TB):
                    hs = h_tm[:, b, j * CW:(j + 1) * CW]
                    dve.tensor_tensor(hs, hs, acc[ch.bank][:, b, :], ALU.add).then_inc(h_step if b == 0 else chunk_free[ch.bank], 1)

            cut(out_chunk(0).unit + RING, UPC - RING)
            dve.wait_ge(h_loaded, 32)
            for j in range(1, 4):
                cut_chunk(out_chunk(j), {3: [lambda: add_to_h(out_chunk(j - 1), j - 1)]})
            add_to_h(out_chunk(3), 3)
            statistics(1, h_tm, u2)
            stationary(2, C_N2)

            def cut_h(half, j, pair=None):
                q = Lin(j).along(8, half)
                tiles = cut_at(j, 4)
                if pair is not None:
                    q = q.along(2, pair)
                    tiles = bass.ds(pair * 8 + 4 * j, 4)

                def run():
                    dve.wait_ge(hT_hi_done, (q + 1).val())
                    dve.tensor_tensor(hT_lo[:, tiles, :], relu2[:, :, :], hT_hi[:, tiles, :], ALU.subtract).then_inc(hT_lo_done, 1)
                return {6: [run]}

            with dve.Fori(0, 2) as half:
                cut_chunk(up_chunk(half, 0))
                with dve.Fori(0, 3) as pair:
                    cut_chunk(up_chunk(half, 1, pair), cut_h(half, 0, pair))
                    cut_chunk(up_chunk(half, 2, pair), cut_h(half, 1, pair))
                cut_chunk(up_chunk(half, 7), cut_h(half, 6))
                cut_chunk(down_chunk(half, 0), cut_h(half, 7))
                for j in range(1, 4):
                    cut_chunk(down_chunk(half, j), {3: [lambda: add_to_h(down_chunk(half, j - 1), j - 1)]})
                add_to_h(down_chunk(half, 3), 3)
            statistics(2, h_tm, None)
            dve.wait_ge(fw_loaded, 16)
            for b in range(TB):
                dve.scalar_tensor_tensor(u2[:, b, :], h_tm[:, b, :], stat[:, 10 + b:11 + b], fw[:, :],
                                         ALU.mult, ALU.mult).then_inc(out_ready, 1)

        @block.tensor
        def _(pe):
            def start_chunk(ch):
                if ch.turn.c > 0:
                    pe.wait_ge(chunk_free[ch.bank], ch.turn.val())

            def token_major(ch, hi, lo, hooks=None):
                nk = ch.units * KPU
                start_chunk(ch)
                for u in range(ch.units):
                    for hook in (hooks or {}).get(u, ()):
                        hook()
                    m = ch.unit + u
                    slot = m.mod(RING)
                    pe.wait_ge(lo_ready, (m + 1).val())
                    for kk in range(KPU):
                        k = u * KPU + kk
                        wh, wl = (w[:, slot, kk * CW:(kk + 1) * CW] for w in (w_hi, w_lo))
                        for b in range(TB):
                            bs = slice(b * P, (b + 1) * P)
                            o = acc[ch.bank][:, b, :]
                            pe.matmul(o, hi[:, k, bs], wh, start=(k == 0), stop=False)
                            pe.matmul(o, hi[:, k, bs], wl, start=False, stop=False)
                            mm = pe.matmul(o, lo[:, k, bs], wh, start=False, stop=(k == nk - 1))
                    mm.then_inc(unit_used, 1)

            def feature_major(ch, hooks=None):
                start_chunk(ch)
                for u in range(ch.units):
                    for hook in (hooks or {}).get(u, ()):
                        hook()
                    m = ch.unit + u
                    slot = m.mod(RING)
                    pe.wait_ge(lo_ready, (m + 1).val())
                    for kk in range(KPU):
                        k = u * KPU + kk
                        for t in range(4):
                            ws = slice(kk * CW + t * P, kk * CW + (t + 1) * P)
                            o = acc[ch.bank][:, t // 2, (t % 2) * T:(t % 2 + 1) * T]
                            pe.matmul(o, w_hi[:, slot, ws], st_hi[:, k, :], start=(k == 0 and t % 2 == 0), stop=False, skip_group_check=True)
                            pe.matmul(o, w_hi[:, slot, ws], st_lo[:, k, :], start=False, stop=False, skip_group_check=True)
                            mm = pe.matmul(o, w_lo[:, slot, ws], st_hi[:, k, :], start=False, stop=(k == KT - 1), skip_group_check=True)
                    mm.then_inc(unit_used, 1)

            def transposes(r, src):
                for kp in range(KT // 2):
                    if kp >= 4:
                        pe.wait_ge(st_lo_done, KT * r + 2 * (kp - 3))
                    for j in range(2):
                        for b in range(TB):
                            k = 2 * kp + j
                            mm = pe.transpose(mp[:, kp % 4, j * T + b * P:j * T + (b + 1) * P], src[:, b, k * P:(k + 1) * P], ident)
                    mm.then_inc(tr_done, 1)
                pe.wait_ge(st_lo_done, KT * (r + 1))

            pe.wait_ge(small_loaded, 32)
            pe.wait_ge(xn_ready, 2)
            transposes(0, x_tm)

            for u in range(DT_UNITS):
                pe.wait_ge(lo_ready, u + 1)
                for kk in range(UE // P):
                    k = u * (UE // P) + kk
                    ws = slice(kk * P, (kk + 1) * P)
                    o = mp[:, 0, 0:T]
                    pe.matmul(o, w_hi[:, u, ws], st_hi[:, k, :], start=(k == 0), stop=False)
                    pe.matmul(o, w_hi[:, u, ws], st_lo[:, k, :], start=False, stop=False)
                    mm = pe.matmul(o, w_lo[:, u, ws], st_hi[:, k, :], start=False, stop=(k == KT - 1))
                mm.then_inc(unit_used, 1)
            pe.wait_ge(table_loaded, 32)
            pe.matmul(mp[0:ATT_H, 3, 0:LINE], relt_sb, onehot_sb, start=True, stop=True).then_inc(line_done, 1)

            feature_major(K_CHUNK)

            def dt_transposes():
                pe.wait_ge(dt_ready, 1)
                for n, tile in enumerate((8, 9)):
                    for blk in range(TB):
                        mm = pe.transpose(mp[:, 2, (2 * n + blk) * SSM_H:(2 * n + blk + 1) * SSM_H],
                                          dtw[:, tile, blk * P:(blk + 1) * P], ident[0:SSM_H, 0:SSM_H])
                mm.then_inc(dtT_done, 1)

            token_major(V_CHUNK, st_hi, st_lo)
            feature_major(bc_chunk(0), {3: [dt_transposes]})
            for j in range(1, 4):
                feature_major(bc_chunk(j))
            feature_major(q_chunk(0))

            def cb_products(groups):
                def run():
                    pe.wait_ge(silu_done, 4)
                    pe.wait_ge(tmcols_ready, 1)
                    pe.wait_ge(line_copied, 1)
                    for g in groups:
                        if g >= 4:
                            pe.wait_ge(cbm_ready, g - 3)
                        b_, c_ = bc[:, g, :], bc[:, SSM_G + g, :]
                        pe.matmul(mp[:, g % 4, 0:T], b_[:, 0:P], c_, start=True, stop=True)
                        pe.matmul(mp[:, g % 4, T:SW], b_[:, P:T], c_[:, P:T], start=True, stop=True).then_inc(cb_done, 1)
                return [run]

            feature_major(q_chunk(1), {1: cb_products(range(4)), 6: cb_products(range(4, 8))})
            feature_major(q_chunk(2))
            feature_major(q_chunk(3))
            feature_major(x_chunk(0))
            pe.wait_ge(cbm_ready, SSM_G)

            def group(g):
                it = at(0, 1, g)

                def scores_ready():
                    pe.wait_ge(qkv_ready, at(3, 3, g).val())

                def scores():
                    for b in range(TB):
                        for h in range(4):
                            ps = slice((h % 2) * HD, (h % 2 + 1) * HD)
                            for e in range(2):
                                c = 2 * b + e
                                at_ = (2 * b + h // 2) * WIN
                                mm = pe.matmul(mp[e * L:(e + 1) * L, h % 2, at_:at_ + WIN],
                                               q_g[ps, h // 2, c * L:(c + 1) * L], k_g[ps, c * L:c * L + WIN], start=True, stop=True)
                    mm.then_inc(scores_done, 1)

                def x_transposes():
                    pe.wait_ge(silu_done, (it + 5).val())
                    for blk in range(TB):
                        for t in range(4):
                            mm = pe.transpose(mp[:, 2 + blk, t * P:(t + 1) * P], x_fm[:, t, blk * P:(blk + 1) * P], ident)
                    mm.then_inc(xT_done, 1)

                def p_transposes():
                    pe.wait_ge(probs_ready, (it + 1).val())
                    for b in range(TB):
                        for h in range(4):
                            hs = slice(h * WIN, (h + 1) * WIN)
                            mm = pe.transpose(mp[:, b, hs], probs[:, b, hs], ident)
                    mm.then_inc(pT_done, 1)

                def ssd():
                    pe.wait_ge(xdt_ready, at(2, 2, g).val())
                    pe.wait_ge(mix_ready, at(2, 2, g).val())
                    for h in range(HPG):
                        t, hp = h // 2, slice((h % 2) * HD, (h % 2 + 1) * HD)
                        hs = slice(h * HD, (h + 1) * HD)
                        d = dec[h // 4][:, h % 4, :]
                        o = mp[hp, 2 + t // 2, (t % 2) * T:(t % 2 + 1) * T]
                        pe.matmul(o, xdt[:, 0, hs], d[:, 0:T], start=True, stop=False)
                        mm = pe.matmul(o[:, P:T], xdt[:, 1, hs], d[:, T:SW], start=False, stop=True)
                    mm.then_inc(y_done, 1)

                def weighted_values():
                    pe.wait_ge(pT_copied, (it + 1).val())
                    for c in range(NCH):
                        for e in range(2):
                            o = mp[e * HD:(e + 1) * HD, 0, :].rearrange("p (t q) -> p t q", t=2)[:, :, c * L:(c + 1) * L]
                            pt = probsT[:, e, :].rearrange("p (b t q) -> p b t q", b=2, t=2)[:, c // 2, :, (c % 2) * L:(c % 2 + 1) * L]
                            mm = pe.matmul(o, v_g[:, c, :], pt, start=True, stop=True)
                    mm.then_inc(pv_done, 1)

                def sums_of_squares():
                    pe.wait_ge(folded, (it + 1).val())
                    pe.matmul(mp[:, 1, 0:T], ones, sq[:, 0, :], start=True, stop=True).then_inc(sumsq_done, 1)

                def banks_read():
                    pe.wait_ge(att_copied, (it + 1).val())
                    pe.wait_ge(ms_ready, (it + 1).val())

                return {2: [scores_ready], 3: [scores], 5: [x_transposes], 8: [ssd], 11: [p_transposes], 13: [weighted_values],
                        14: [sums_of_squares], 18: [banks_read]}

            feature_major(z_chunk(0), part(group(0), 0))
            with pe.Fori(0, SSM_G - 1) as g:
                feature_major(next_x(g), part(group(g), UPC))
                feature_major(next_z(g), joined(part(group(g), 2 * UPC), part(group(g + 1), 0)))
            token_major(ga_chunk(0), st_hi, st_lo, part(group(SSM_G - 1), UPC))

            token_major(gb_chunk(0), st_hi, st_lo)

            def merge(j, last):
                token_major(ssm_chunk(j), y_hi, y_lo, {2 * p: [lambda p=p: pe.wait_ge(y_lo_done, p + 1)] for p in range(8)})
                pe.wait_ge(att_lo_done, 4)
                token_major(att_chunk(j), att_hi, att_lo)
                if not last:
                    token_major(next_ga(j), st_hi, st_lo)
                    token_major(next_gb(j), st_hi, st_lo)

            with pe.Fori(0, 3) as j:
                merge(j, False)
            merge(3, True)

            pe.wait_ge(mg_done, 8)
            transposes(1, merged)
            for j in range(4):
                token_major(out_chunk(j), st_hi, st_lo)

            pe.wait_ge(xn_ready, 4)
            transposes(2, u2)
            with pe.Fori(0, 2) as half:
                with pe.Fori(0, 4) as pair:
                    for j in range(2):
                        feature_major(up_chunk(half, j, pair))

                def all_h():
                    pe.wait_ge(hT_lo_done, at(8, 8, half).val())
                pe.wait_ge(hT_lo_done, at(7, 8, half).val())
                for j in range(4):
                    token_major(down_chunk(half, j), hT_hi, hT_lo, {14: [all_h]} if j == 0 else None)


def _t5_bucket(rel):
    nb = BUCKETS // 2
    ret = (rel > 0).astype(np.int32) * nb
    n = np.abs(rel)
    exact = nb // 2
    large = exact + (np.log(np.maximum(n, 1) / exact) / np.log(MAX_DIST / exact) * (nb - exact)).astype(np.int32)
    large = np.minimum(large, nb - 1)
    return (ret + np.where(n < exact, n, large)).astype(np.int32)


def kernel(x, rel_table, norm1_w, w_in, conv_w, conv_b, dt_bias, a_log, d_skip, ssm_norm_w, sinks,
           w_proj_ssm, w_proj_attn, w_out, norm2_w, w_up, w_down, final_norm_w):
    import concourse.bacc as _bacc
    from concourse.bass_utils import run_bass_kernel_spmd as _run

    def tiles(v):
        return np.asarray(v).reshape(-1, P).T

    def column(v):
        full = np.zeros((P, 1), np.float32)
        full[:SSM_H, 0] = np.asarray(v)
        return full

    cw = np.asarray(conv_w)[0].reshape(4, CONV_T, P).transpose(2, 1, 0).reshape(P, 4 * CONV_T)
    cols = np.concatenate([
        cw, tiles(conv_b[0]), tiles(norm1_w[0]), tiles(norm2_w[0]), tiles(ssm_norm_w[0]),
        tiles(np.repeat(np.asarray(d_skip)[0], HD)), np.broadcast_to(np.asarray(sinks)[0], (P, ATT_H)),
        column(dt_bias[0]), column(a_log[0])], axis=1)
    tri = np.triu(np.ones((P, P), np.float32))
    one = np.ones((P, P), np.float32)
    consts = np.concatenate([np.eye(P, dtype=np.float32), tri, one, tri, one], axis=1)
    onehot = np.zeros((BUCKETS, LINE), np.float32)
    rel = np.arange(LINE - 1) - (WIN - 1)
    onehot[_t5_bucket(rel), np.arange(LINE - 1)] = 1.0

    given = {
        "x": np.asarray(x)[0], "w_in": np.asarray(w_in)[0], "w_ssm": np.asarray(w_proj_ssm)[0],
        "w_att": np.asarray(w_proj_attn)[0], "w_out": np.asarray(w_out)[0], "w_up": np.asarray(w_up)[0],
        "w_down": np.asarray(w_down)[0], "rel_table": np.asarray(rel_table), "fnorm": np.asarray(final_norm_w),
        "cols_in": cols, "consts_in": consts, "onehot_in": onehot,
    }
    nc = _bacc.Bacc("TRN2", target_bir_lowering=False, num_devices=1)
    arrays, args = {}, []
    for name, a in given.items():
        a = np.ascontiguousarray(a)
        arrays[f"in_{name}"] = a
        args.append(nc.dram_tensor(f"in_{name}", a.shape, mybir.dt.from_np(a.dtype), kind="ExternalInput").ap())
    args.append(nc.dram_tensor("out_0", (T, D), F32, kind="ExternalOutput").ap())
    build(nc, *args)
    r = _run(nc, [arrays], core_ids=[0])
    return r.results[0]["out_0"].reshape(1, T, D)
```

```python
from contextlib import ExitStack

import numpy as np
import concourse.bass as bass
from concourse import mybir

F32 = mybir.dt.float32
F32R = mybir.dt.float32r
ALU = mybir.AluOpType
ACT = mybir.ActivationFunctionType
AX = mybir.AxisListType

P = 128
T = 256
TB = T // P
D = 2048
DI = 4096
L = 64
NCH = T // L
SSM_H, SSM_G, NST = 64, 8, 128
HPG = SSM_H // SSM_G
ATT_H, KV, HD = 32, 8, 64
WIN = 2 * L
BUCKETS, MAX_DIST = 32, 128
DFF = 8192
EPS = 1e-6

Z_OFF = 0
XBC_OFF = DI
CONV_DIM = DI + 2 * SSM_G * NST
DT_OFF = XBC_OFF + CONV_DIM
Q_OFF = DT_OFF + SSM_H
K_OFF = Q_OFF + ATT_H * HD
V_OFF = K_OFF + KV * HD
GA_OFF = V_OFF + KV * HD
GB_OFF = GA_OFF + D

CW = 512
KT = D // P
KPU = 2
UPC = KT // KPU
RING = 4
UE = KPU * CW
MAIN, LAST = (slice(0, 3 * CW // 2), slice(3 * CW // 2, 3 * CW)), slice(3 * CW, D)
MASKED = -1.0e30

CONV_T = CONV_DIM // P
C_CONVW = 0
C_CONVB = C_CONVW + 4 * CONV_T
C_N1 = C_CONVB + CONV_T
C_N2 = C_N1 + KT
C_SSMN = C_N2 + KT
C_SKIP = C_SSMN + DI // P
C_SINK = C_SKIP + DI // P
C_DTB = C_SINK + ATT_H // 2
C_ALOG = C_DTB + 1
C_ALL = C_ALOG + 1
K_ID = 0
K_MASK = K_ID + P
SW = 3 * P
K_ONES = K_MASK + SW
K_ALL = K_ONES + P
LINE = 192


class Lin:

    def __init__(self, c, terms=()):
        self.c, self.terms = c, tuple(terms)

    def __add__(self, k):
        return Lin(self.c + k, self.terms)

    def along(self, coef, reg):
        return Lin(self.c, self.terms + ((coef, reg),))

    def over(self, d):
        assert all(k % d == 0 for k, _ in self.terms)
        return Lin(self.c // d, [(k // d, r) for k, r in self.terms])

    def times(self, m):
        return Lin(self.c * m, [(k * m, r) for k, r in self.terms])

    def mod(self, d):
        assert all(k % d == 0 for k, _ in self.terms)
        return self.c % d

    def val(self):
        v = self.c
        for k, r in self.terms:
            v = r * k + v
        return v


def at(base, step, i):
    return Lin(base + step * i) if isinstance(i, int) else Lin(base).along(step, i)


def cut_at_off(i, size, off):
    return slice(off + i * size, off + (i + 1) * size) if isinstance(i, int) else bass.ds(i * size + off, size)


def cut_at(i, size):
    return slice(i * size, (i + 1) * size) if isinstance(i, int) else bass.ds(i * size, size)


class Chunk:

    def __init__(self, unit, units, number):
        self.unit = unit
        self.units = units
        self.end = unit + units
        self.bank = number.mod(2)
        self.turn = number.over(2)
        self.left = self.turn + 1


DT_UNITS = 2
U_K = DT_UNITS
U_V, U_BC = U_K + UPC, U_K + 2 * UPC
U_Q = U_BC + 4 * UPC
U_X = U_Q + 4 * UPC
U_MERGE = U_X + 18 * UPC
MERGE_U = 5 * UPC
U_OUT = U_MERGE + 4 * MERGE_U - 2 * UPC
U_MLP = U_OUT + 4 * UPC
HALF_U = 8 * UPC + 4 * 2 * UPC
N_BC, N_Q, N_X, N_MERGE, N_OUT, N_MLP, HALF_N = 2, 6, 10, 28, 42, 46, 12

K_CHUNK, V_CHUNK = Chunk(Lin(U_K), UPC, Lin(0)), Chunk(Lin(U_V), UPC, Lin(1))


def q_chunk(j):
    return Chunk(at(U_Q, UPC, j), UPC, at(N_Q, 1, j))


def bc_chunk(j):
    return Chunk(at(U_BC, UPC, j), UPC, at(N_BC, 1, j))


def x_chunk(g):
    return Chunk(at(U_X, 2 * UPC, g), UPC, at(N_X, 2, g))


def z_chunk(g):
    return Chunk(at(U_X + UPC, 2 * UPC, g), UPC, at(N_X + 1, 2, g))


def ga_chunk(j):
    return Chunk(at(U_MERGE - 2 * UPC, MERGE_U, j), UPC, at(N_MERGE - 2, 4, j))


def gb_chunk(j):
    return Chunk(at(U_MERGE - UPC, MERGE_U, j), UPC, at(N_MERGE - 1, 4, j))


def ssm_chunk(j):
    return Chunk(at(U_MERGE, MERGE_U, j), 2 * UPC, at(N_MERGE, 4, j))


def att_chunk(j):
    return Chunk(at(U_MERGE + 2 * UPC, MERGE_U, j), UPC, at(N_MERGE + 1, 4, j))


def is_last(g):
    return isinstance(g, int) and g == SSM_G - 1


def next_x(g):
    return Chunk(at(U_X + 2 * UPC, 2 * UPC, g), UPC, at(N_X + 2, 2, g))


def next_z(g):
    return Chunk(at(U_X + 3 * UPC, 2 * UPC, g), UPC, at(N_X + 3, 2, g))


def part(steps, first):
    return {place - first: run for place, run in steps.items() if first <= place < first + UPC}


def joined(a, b):
    return {u: a.get(u, []) + b.get(u, []) for u in sorted({*a, *b})}


def next_ga(j):
    return Chunk(at(U_MERGE + 3 * UPC, MERGE_U, j), UPC, at(N_MERGE + 2, 4, j))


def next_gb(j):
    return Chunk(at(U_MERGE + 4 * UPC, MERGE_U, j), UPC, at(N_MERGE + 3, 4, j))


def out_chunk(j):
    return Chunk(Lin(U_OUT + j * UPC), UPC, Lin(N_OUT + j))


def up_chunk(half, j, pair=None):
    unit = at(U_MLP + j * UPC, HALF_U, half)
    number = at(N_MLP + j, HALF_N, half)
    if pair is not None:
        unit, number = unit.along(2 * UPC, pair), number.along(2, pair)
    return Chunk(unit, UPC, number)


def down_chunk(half, j):
    return Chunk(at(U_MLP + (8 + 2 * j) * UPC, HALF_U, half), 2 * UPC, at(N_MLP + 8 + j, HALF_N, half))


def build(nc, x, w_in, w_ssm, w_att, w_out, w_up, w_down, rel_table, fnorm, cols_in, consts_in, onehot_in, out):
    decay_rows = nc.dram_tensor("decay_rows", (2, SSM_H, SW), F32).ap()
    bias_skew = nc.dram_tensor("bias_skew", (ATT_H, L, LINE), F32).ap()

    ctx = ExitStack()
    with ctx:
        def sb(name, shape, dt=F32, stack=ctx):
            return stack.enter_context(nc.sbuf_tensor(name, shape, dt))

        def sem(name):
            return ctx.enter_context(nc.semaphore(name))

        raw = sb("raw", [P, RING, UE])
        w_hi = sb("w_hi", [P, RING, UE], F32R)
        w_lo = sb("w_lo", [P, RING, UE], F32R)
        cols = sb("cols", [P, C_ALL])
        consts = sb("consts", [P, K_ALL])
        stat = sb("stat", [P, 24])
        sums = stat[:, 0:8].rearrange("p (b n) -> p b n", b=TB)
        ms, root, rstd_1, newton, rstd, rstd_sq = (stat[:, n:n + TB] for n in range(8, 20, 2))
        ident = consts[:, K_ID:K_ID + P]
        mask = consts[:, K_MASK:K_MASK + SW]
        ones = consts[:, K_ONES:K_ONES + P]

        front = ExitStack()
        st_hi = sb("st_hi", [P, KT, T], F32R, stack=front)
        st_lo = sb("st_lo", [P, KT, T], F32R, stack=front)

        mix = ExitStack()
        y32 = sb("y32", [P, 32, T], stack=mix)
        qatt = sb("qatt", [P, KT, T], stack=mix)
        kdup = sb("kdup", [P, KV, L + T], stack=mix)
        v_win = sb("v_win", [P, NCH, CW], stack=mix)
        bias_g = sb("bias_g", [P, 2, WIN], stack=mix)
        cbm = sb("cbm", [P, SSM_G, SW], stack=mix)
        dec = [sb(f"dec{n}", [P, 4, SW], stack=mix) for n in range(2)]
        xraw = sb("xraw", [P, 4, 3 + T], stack=mix)
        xc = sb("xc", [P, 4, T], stack=mix)
        x_fm = sb("x_fm", [P, 4, T], stack=mix)
        xdt = sb("xdt", [P, TB, CW], stack=mix)
        probs = sb("probs", [P, TB, CW], stack=mix)
        probsT = sb("probsT", [P, TB, CW], stack=mix)
        tmcols = sb("tmcols", [P, 4, SSM_H], stack=mix)
        q_g = sb("q_g", [P, NCH, 2 * L], stack=mix)
        k_g = sb("k_g", [P, L + T], stack=mix)
        v_g = sb("v_g", [P, NCH, HD], stack=mix)
        cb_g = sb("cb_g", [P, SW], stack=mix)
        smx = sb("smx", [P, 4, 8], stack=mix)
        mix.close()
        x_tm = y32[:, 0:16, :].rearrange("p (b j) t -> p b (j t)", b=TB)
        bc = y32[:, 0:16, :]
        dtw = y32[0:SSM_H, 16:32, :]
        unread_x = y32[:, 16:20, :].rearrange("p j t -> p (j t)")
        line_sb = y32[0:ATT_H, 31, 0:LINE]
        relt_sb = y32[0:BUCKETS, 30, 0:ATT_H]
        onehot_sb = y32[0:BUCKETS, 30, ATT_H:ATT_H + LINE]
        zs = xc
        sq = xdt[:, :, :].rearrange("p b (j t) -> p (b j) t", t=T)
        ms_g, rstd_g = sq[:, 2, :], sq[:, 3, :]

        mrg = ExitStack()
        y_lo = sb("y_lo", [P, 32, T], F32R, stack=mrg)
        att_lo = sb("att_lo", [P, KT, T], F32R, stack=mrg)
        sga = sb("sga", [P, TB, CW], stack=mrg)
        sgb = sb("sgb", [P, TB, CW], stack=mrg)
        y_hi = sb("y_hi", [P, 32, T], F32R, stack=mrg)
        att_hi = sb("att_hi", [P, KT, T], F32R, stack=mrg)
        merged = sb("merged", [P, TB, D], stack=mrg)
        mrg.close()
        front.close()

        mlp = ExitStack()
        relu = sb("relu", [P, 4, T], stack=mlp)
        relu2 = sb("relu2", [P, 4, T], stack=mlp)
        fw = sb("fw", [P, D], stack=mlp)
        out_sb = sb("out_sb", [P, TB, D], stack=mlp)
        h_tm = sb("h_tm", [P, TB, D], stack=mlp)
        up_hi = sb("up_hi", [P, KT, T], F32R, stack=mlp)
        up_lo = sb("up_lo", [P, KT, T], F32R, stack=mlp)
        hT_hi = sb("hT_hi", [P, 32, T], F32R, stack=mlp)
        hT_lo = sb("hT_lo", [P, 32, T], F32R, stack=mlp)
        mlp.close()

        acc = [ctx.enter_context(nc.psum_tensor(f"acc{n}", [P, 2, 512], F32)) for n in range(2)]
        mp = ctx.enter_context(nc.psum_tensor("mp", [P, 4, 512], F32))

        loaded = [sem(f"loaded{n}") for n in range(RING)]
        hi_ready, lo_ready, unit_used = sem("hi_ready"), sem("lo_ready"), sem("unit_used")
        chunk_free = [sem(f"chunk_free{n}") for n in range(2)]
        x_loaded = [sem(f"x_loaded{n}") for n in range(2 * TB)]
        small_loaded, one_set = sem("small_loaded"), sem("one_set")
        table_loaded = sem("table_loaded")
        ss_ready, stat_step, rstd_ready = sem("ss_ready"), sem("stat_step"), sem("rstd_ready")
        x_scaled = [sem(f"x_scaled{half}") for half in range(2)]
        root_ready, rstd_sq_ready = sem("root_ready"), sem("rstd_sq_ready")
        tr_done, st_hi_done, st_lo_done = sem("tr_done"), sem("st_hi_done"), sem("st_lo_done")
        dt_step, dt_act, dt_ready = sem("dt_step"), sem("dt_act"), sem("dt_ready")
        dtT_done, tmcols_ready, rows_stored = sem("dtT_done"), sem("tmcols_ready"), sem("rows_stored")
        line_done, line_copied, skew_stored = sem("line_done"), sem("line_copied"), sem("skew_stored")
        pads_ready, kv_copied, kv_spread = sem("pads_ready"), sem("kv_copied"), sem("kv_spread")
        conv_step, conv_done, silu_done = sem("conv_step"), sem("conv_done"), sem("silu_done")
        cb_done, cbm_ready = sem("cb_done"), sem("cbm_ready")
        dec_loaded, clamped, dec_exp, mix_ready = sem("dec_loaded"), sem("clamped"), sem("dec_exp"), sem("mix_ready")
        bias_loaded = sem("bias_loaded")
        scores_done, sm_step, shifted, exped = sem("scores_done"), sem("sm_step"), sem("shifted"), sem("exped")
        probs_ready, pT_done, pT_copied = sem("probs_ready"), sem("pT_done"), sem("pT_copied")
        pv_done, att_copied = sem("pv_done"), sem("att_copied")
        xT_done, xdt_ready, y_done = sem("xT_done"), sem("xdt_ready"), sem("y_done")
        gate_step, gated, squared, sumsq_done = sem("gate_step"), sem("gated"), sem("squared"), sem("sumsq_done")
        cb_step, fold_step, folded = sem("cb_step"), sem("fold_step"), sem("folded")
        gn_step, ms_ready, gn_ln, rstd0_ready, y_out = sem("gn_step"), sem("ms_ready"), sem("gn_ln"), sem("rstd0_ready"), sem("y_out")
        y_hi_done, y_lo_done, att_lo_done = sem("y_hi_done"), sem("y_lo_done"), sem("att_lo_done")
        qkv_ready, mg_step, mg_done = sem("qkv_ready"), sem("mg_step"), sem("mg_done")
        h_loaded, h_step, fw_loaded = sem("h_loaded"), sem("h_step"), sem("fw_loaded")
        relu_sq, hT_hi_done, hT_lo_done = sem("relu_sq"), sem("hT_hi_done"), sem("hT_lo_done")
        fw_applied, out_ready_act, out_ready_dve, stored = sem("fw_applied"), sem("out_ready_act"), sem("out_ready_dve"), sem("stored")

        def spread(ap, *dims):
            return bass.AP(ap.tensor, ap.offset, [list(ap.ap[0])] + [list(d) for d in dims])

        block = ctx.enter_context(nc.Block())

        @block.sync
        def _(sp):
            for b in range(TB):
                for half in range(2):
                    cs = cut_at(half, D // 2)
                    sp.dma_start(x_tm[:, b, cs], x[b * P:(b + 1) * P, cs]).then_inc(x_loaded[2 * b + half], 16)
            sp.dma_start(cols[:, :], cols_in).then_inc(small_loaded, 16)
            sp.dma_start(consts[:, :], consts_in).then_inc(small_loaded, 16)

            def unit(n, src):
                slot = n.mod(RING)
                if n.c >= RING:
                    sp.wait_ge(lo_ready, (n + (1 - RING)).val())
                sp.dma_start(raw[:, slot, :].rearrange("p (k c) -> p k c", k=src.shape[1]), src).then_inc(loaded[slot], 16)

            def chunk(ch, w, col, row0=0):
                for u in range(ch.units):
                    r = row0 + u * KPU * P
                    rows = w[r:r + KPU * P] if isinstance(r, int) else w[bass.ds(r, KPU * P)]
                    src = rows[:, col:col + CW] if isinstance(col, int) else rows[:, bass.ds(col, CW)]
                    unit(ch.unit + u, src.rearrange("(k p) c -> p k c", p=P))

            for u in range(DT_UNITS):
                unit(Lin(u), w_in[u * (D // 2):(u + 1) * (D // 2), DT_OFF:DT_OFF + P].rearrange("(k p) c -> p k c", p=P))
            chunk(K_CHUNK, w_in, K_OFF)
            chunk(V_CHUNK, w_in, V_OFF)
            for j in range(4):
                chunk(bc_chunk(j), w_in, XBC_OFF + DI + j * CW)
            for j in range(4):
                chunk(q_chunk(j), w_in, Q_OFF + j * CW)
            chunk(x_chunk(0), w_in, XBC_OFF)
            chunk(z_chunk(0), w_in, Z_OFF)
            with sp.Fori(0, SSM_G - 1) as g:
                chunk(next_x(g), w_in, g * CW + (XBC_OFF + CW))
                chunk(next_z(g), w_in, g * CW + (Z_OFF + CW))
            chunk(ga_chunk(0), w_in, GA_OFF)
            chunk(gb_chunk(0), w_in, GB_OFF)
            with sp.Fori(0, 3) as j:
                chunk(ssm_chunk(j), w_ssm, j * CW)
                chunk(att_chunk(j), w_att, j * CW)
                chunk(next_ga(j), w_in, j * CW + (GA_OFF + CW))
                chunk(next_gb(j), w_in, j * CW + (GB_OFF + CW))
            chunk(ssm_chunk(3), w_ssm, 3 * CW)
            chunk(att_chunk(3), w_att, 3 * CW)
            for j in range(4):
                chunk(out_chunk(j), w_out, j * CW)
            with sp.Fori(0, 2) as half:
                with sp.Fori(0, 4) as pair:
                    for j in range(2):
                        chunk(up_chunk(half, j, pair), w_up, half * (8 * CW) + (pair * (2 * CW) + j * CW))
                for j in range(4):
                    chunk(down_chunk(half, j), w_down, j * CW, half * (DFF // 2))
            for ready, count, b, cs in ((out_ready_dve, 1, 0, LAST), (out_ready_act, 1, 0, MAIN[0]), (out_ready_dve, 2, 1, LAST),
                                        (out_ready_act, 2, 0, MAIN[1]), (out_ready_dve, 3, 1, MAIN[0]), (out_ready_dve, 4, 1, MAIN[1])):
                sp.wait_ge(ready, count)
                sp.dma_start(out[b * P:(b + 1) * P, cs], out_sb[:, b, cs]).then_inc(stored, 16)
            sp.wait_ge(stored, 16 * 6)

        @block.gpsimd
        def _(pool):
            pool.memset(stat[:, 20:21], 1.0).then_inc(one_set, 1)
            pool.memset(kdup[:, :, 0:L], 0.0).then_inc(pads_ready, 1)
            pool.memset(v_win[0:L, 0, :], 0.0).then_inc(pads_ready, 1)
            pool.memset(xraw[:, :, 0:3], 0.0).then_inc(pads_ready, 1)

            def group_qkv(g):
                pool.tensor_copy(q_g[:, :, :].rearrange("p c (t q) -> p c t q", t=2),
                                 qatt[:, cut_at(g, 2), :].rearrange("p t (c q) -> p c t q", q=L)).then_inc(qkv_ready, 1)
                pool.tensor_copy(k_g[:, :], kdup[:, cut_at(g, 1), :].rearrange("p a t -> p (a t)")).then_inc(qkv_ready, 1)
                pool.tensor_copy(v_g[:, :, :], v_win[:, :, cut_at(g, HD)]).then_inc(qkv_ready, 1)

            def group(g):
                it = at(0, 1, g)
                pool.wait_ge(dec_exp, (it.times(2) + 2).val())
                pool.tensor_copy(cb_g[:, :], cbm[:, cut_at(g, 1), :].rearrange("p a t -> p (a t)")).then_inc(cb_step, 1)
                pool.wait_ge(cb_step, (it + 1).val())
                for k in range(2):
                    pool.tensor_tensor(dec[k][:, :, :], dec[k][:, :, :], spread(cb_g[:, :], (0, 4), (1, SW)), ALU.mult).then_inc(mix_ready, 1)
                pool.wait_ge(squared, (it + 1).val())
                pool.tensor_tensor(sq[:, 0:2, :], sq[:, 0:2, :], sq[:, 2:4, :], ALU.add).then_inc(fold_step, 1)
                pool.wait_ge(fold_step, (it + 1).val())
                pool.tensor_tensor(sq[:, 0, :], sq[:, 0, :], sq[:, 1, :], ALU.add).then_inc(folded, 1)

            pool.wait_ge(chunk_free[1], q_chunk(3).left.val())
            pool.wait_ge(cbm_ready, SSM_G)
            pool.wait_ge(kv_spread, 64)
            group_qkv(0)
            with pool.Fori(0, SSM_G - 1) as g:
                group(g)
                pool.wait_ge(pv_done, g + 1)
                group_qkv(g + 1)
            group(SSM_G - 1)

            for p in range(4):
                pool.wait_ge(y_hi_done, 8 + p + 1)
                s = cut_at(p, 4)
                pool.tensor_tensor(att_lo[:, s, :], qatt[:, s, :], att_hi[:, s, :], ALU.subtract).then_inc(att_lo_done, 1)

            pool.wait_ge(fw_loaded, 16)
            for j in range(3):
                ch, cs = down_chunk(1, j), cut_at(j, CW)
                pool.wait_ge(chunk_free[ch.bank], ch.left.val())
                for b in range(TB):
                    pool.tensor_tensor(out_sb[:, b, cs], h_tm[:, b, cs], fw[:, cs], ALU.mult).then_inc(fw_applied, 1)

        @block.scalar
        def _(act):
            def cut(n, count, steps=None):
                for u in range(count):
                    for run in (steps or {}).get(u, ()):
                        run()
                    m = n + u
                    slot = m.mod(RING)
                    act.wait_ge(loaded[slot], (m.over(RING) + 1).times(16).val())
                    if m.c >= RING:
                        act.wait_ge(unit_used, (m + (1 - RING)).val())
                    act.activation(w_hi[:, slot, :], raw[:, slot, :], ACT.Copy).then_inc(hi_ready, 1)

            def wait_full(ch):
                act.wait_ge(unit_used, ch.end.val())

            def cut_chunk(ch, steps=None):
                cut(ch.unit, ch.units, steps)

            def squares(before, dst, src, b, n):
                if before:
                    act.wait_ge(ss_ready, before)
                act.activation(dst, src, ACT.Square, accum_out=sums[:, b, n:n + 1]).then_inc(ss_ready, 1)

            def square_root(r):
                act.wait_ge(stat_step, 6 * r + 2)
                act.activation(root, ms, ACT.Sqrt).then_inc(root_ready, 1)

            def stationary(r, kps, wcol, hi):
                for kp in kps:
                    act.wait_ge(tr_done, 8 * r + kp + 1)
                    for j in range(2):
                        k = 2 * kp + j
                        src = mp[:, kp % 4, j * T:(j + 1) * T]
                        scale = 1.0 if wcol is None else cols[:, wcol + k:wcol + k + 1]
                        act.activation(hi[:, k, :], src, ACT.Copy, scale=scale).then_inc(st_hi_done, 1)

            act.dma_start(relt_sb, rel_table).then_inc(table_loaded, 16)
            act.dma_start(onehot_sb, onehot_in).then_inc(table_loaded, 16)
            act.wait_ge(one_set, 1)
            act.activation(stat[:, 21:22], stat[:, 20:21], ACT.Sqrt)
            for b in range(TB):
                for half in range(2):
                    act.wait_ge(x_loaded[2 * b + half], 16)
                    squares(2 * b + half, unread_x, x_tm[:, b, cut_at(half, D // 2)], b, half)
            square_root(0)
            act.wait_ge(rstd_ready, 1)
            xs = x_tm[:, 0, 0:D // 2]
            act.activation(xs, xs, ACT.Copy, scale=rstd[:, 0:1]).then_inc(x_scaled[0], 1)
            act.wait_ge(small_loaded, 32)
            cut(Lin(0), 1)
            stationary(0, range(0, 7), C_N1, st_hi)
            cut(Lin(1), 1)
            stationary(0, range(7, 8), C_N1, st_hi)

            def bias_line():
                act.wait_ge(line_done, 1)
                act.activation(line_sb, mp[0:ATT_H, 3, 0:LINE], ACT.Copy).then_inc(line_copied, 1)
                act.wait_ge(line_copied, 1)
                src = bass.AP(line_sb.tensor, line_sb.offset, [list(line_sb.ap[0]), [0, L], [1, LINE]])
                act.dma_start(bias_skew, src).then_inc(skew_stored, 16)

            def dt_bias():
                act.wait_ge(unit_used, DT_UNITS)
                act.activation(dtw[:, 0, :], acc[1][0:SSM_H, 0, 0:T], ACT.Identity,
                               bias=cols[0:SSM_H, C_DTB:C_DTB + 1]).then_inc(dt_act, 1)
                act.activation(smx[0:SSM_H, 0, 0:1], cols[0:SSM_H, C_ALOG:C_ALOG + 1], ACT.Exp).then_inc(dt_act, 1)

            def dt_exp():
                act.wait_ge(dt_step, 2)
                act.activation(dtw[:, 2, :], dtw[:, 1, :], ACT.Exp).then_inc(dt_act, 1)

            def dt_ln():
                act.wait_ge(dt_step, 3)
                act.activation(dtw[:, 4, :], dtw[:, 3, :], ACT.Ln).then_inc(dt_act, 1)

            def store_rows():
                act.wait_ge(dt_ready, 1)
                rows = dtw[:, 10:13, :].rearrange("h a t -> h (a t)")
                for half in range(2):
                    act.dma_start(decay_rows[half], rows[:, half * SW:(half + 1) * SW]).then_inc(rows_stored, 16)

            def load_decays(g):
                for n in range(2):
                    for half in range(2):
                        first = g * HPG + 4 * n
                        src = decay_rows[half, first:first + 4] if isinstance(first, int) else decay_rows[half, bass.ds(first, 4)]
                        src = bass.AP(src.tensor, src.offset, [[0, L], [SW, 4], [1, SW]])
                        act.dma_start(dec[n][half * L:(half + 1) * L, :, :], src).then_inc(dec_loaded, 16)

            def load_bias(g):
                for t in range(2):
                    heads = g * 4 + 2 * t
                    src = bias_skew[heads:heads + 2] if isinstance(heads, int) else bias_skew[bass.ds(heads, 2)]
                    src = bass.AP(src.tensor, src.offset + (L - 1), [[LINE - 1, L], [L * LINE, 2], [1, WIN]])
                    act.dma_start(bias_g[t * L:(t + 1) * L, :, :], src).then_inc(bias_loaded, 16)

            def banks(ch):
                return acc[ch.bank][:, :, :].rearrange("p b (j t) -> p (b j) t", t=T)

            def keys_out():
                wait_full(K_CHUNK)
                act.wait_ge(pads_ready, 3)
                a = banks(K_CHUNK)
                act.activation(kdup[0:L, 0:KV:2, L:L + T], a[0:L], ACT.Copy).then_inc(kv_copied, 1)
                act.activation(kdup[L:P, 1:KV:2, L:L + T], a[L:P], ACT.Copy).then_inc(chunk_free[0], 1)
                act.wait_ge(kv_copied, 1)
                act.wait_ge(chunk_free[0], K_CHUNK.left.val())
                act.dma_start(kdup[L:P, 0:KV:2, L:L + T], kdup[0:L, 0:KV:2, L:L + T]).then_inc(kv_spread, 16)
                act.dma_start(kdup[0:L, 1:KV:2, L:L + T], kdup[L:P, 1:KV:2, L:L + T]).then_inc(kv_spread, 16)

            def values_out():
                wait_full(V_CHUNK)
                act.activation(v_win[:, 1:NCH:2, :], acc[1][:, :, :], ACT.Copy).then_inc(chunk_free[1], 1)
                act.wait_ge(chunk_free[1], V_CHUNK.left.val())
                act.dma_start(v_win[L:P, 0:NCH:2, :], v_win[0:L, 1:NCH:2, :]).then_inc(kv_spread, 16)
                act.dma_start(v_win[0:L, 2, :], v_win[L:P, 1, :]).then_inc(kv_spread, 16)

            def queries_out(j):
                ch = q_chunk(j)
                wait_full(ch)
                act.activation(qatt[:, 4 * j:4 * j + 4, :], banks(ch), ACT.Copy, scale=HD ** -0.5).then_inc(chunk_free[ch.bank], 1)

            def conv_in(ch):
                wait_full(ch)
                act.activation(xraw[:, :, 3:3 + T], banks(ch), ACT.Copy).then_inc(chunk_free[ch.bank], 1)

            def conv_silu(k, dst):
                act.wait_ge(conv_done, (k + 1).val())
                act.activation(dst, xc[:, :, :], ACT.Silu).then_inc(silu_done, 1)

            cut_chunk(K_CHUNK, {4: [bias_line, dt_bias], 6: [dt_exp]})
            cut_chunk(V_CHUNK, {1: [dt_ln], 3: [keys_out]})
            cut_chunk(bc_chunk(0), {2: [store_rows], 3: [values_out]})
            for j in range(1, 4):
                cut_chunk(bc_chunk(j), {3: [lambda: conv_in(bc_chunk(j - 1))],
                                        6: [lambda: conv_silu(Lin(j - 1), bc[:, 4 * (j - 1):4 * j, :])]})
            cut_chunk(q_chunk(0), {3: [lambda: conv_in(bc_chunk(3))], 6: [lambda: conv_silu(Lin(3), bc[:, 12:16, :])]})
            for j in range(1, 4):
                cut_chunk(q_chunk(j), {3: [lambda: queries_out(j - 1)]})

            def first_loads():
                act.wait_ge(rows_stored, 32)
                load_decays(0)
                act.wait_ge(skew_stored, 16)
                load_bias(0)

            cut_chunk(x_chunk(0), {3: [lambda: queries_out(3)], 4: [first_loads]})

            def group(g):
                it = at(0, 1, g)
                z = z_chunk(g)

                def decay_clamp(k):
                    act.wait_ge(dec_loaded, at(64, 64, g).val())
                    for h in range(4):
                        for blk in range(TB):
                            s = tmcols[:, 2 + blk, cut_at(g * HPG + (4 * k + h), 1)]
                            lo, hi = (0, T) if blk == 0 else (T, SW)
                            ins = act.activation(dec[k][:, h, lo:hi], dec[k][:, h, lo:hi], ACT.Relu, bias=s, scale=-1.0)
                    ins.then_inc(clamped, 1)

                def decay_exp(k):
                    act.wait_ge(clamped, (it.times(2) + (k + 1)).val())
                    act.activation(dec[k][:, :, :], dec[k][:, :, :], ACT.Exp, scale=-1.0).then_inc(dec_exp, 1)

                def softmax_exp():
                    act.wait_ge(shifted, (it.times(2) + 2).val())
                    act.activation(smx[:, 1, :], smx[:, 1, :], ACT.Exp).then_inc(exped, 1)
                    act.activation(probs[:, :, :], probs[:, :, :], ACT.Exp).then_inc(exped, 1)

                def probsT_out():
                    act.wait_ge(pT_done, (it + 1).val())
                    act.activation(probsT[:, :, :], mp[:, 0:2, :], ACT.Copy).then_inc(pT_copied, 1)

                def z_silu():
                    wait_full(z)
                    act.activation(zs[:, :, :], banks(z), ACT.Silu).then_inc(chunk_free[1], 1)

                def square():
                    act.wait_ge(gated, (it + 1).val())
                    act.activation(sq, y32[:, cut_at(g, 4), :], ACT.Square).then_inc(squared, 1)

                def att_out():
                    act.wait_ge(pv_done, (it + 1).val())
                    act.activation(qatt[:, cut_at(g, 2), :], mp[:, 0, :].rearrange("p (j t) -> p j t", j=2),
                                   ACT.Copy).then_inc(att_copied, 1)

                def group_rstd():
                    act.wait_ge(ms_ready, (it + 1).val())
                    act.activation(rstd_g, ms_g, ACT.Ln).then_inc(gn_ln, 1)
                    act.wait_ge(gn_ln, (it + 1).val())
                    act.activation(rstd_g, rstd_g, ACT.Exp, scale=-0.5).then_inc(rstd0_ready, 1)

                def next_bias():
                    act.wait_ge(shifted, (it.times(2) + 2).val())
                    load_bias(g + 1)

                def next_decays():
                    act.wait_ge(y_done, (it + 1).val())
                    load_decays(g + 1)

                steps = {0: [lambda: decay_clamp(0)], 1: [lambda: decay_clamp(1)], 3: [lambda: conv_in(x_chunk(g))],
                         4: [lambda: decay_exp(0)], 5: [lambda: decay_exp(1)],
                         6: [lambda: conv_silu(it + 4, x_fm[:, :, :])], 11: [softmax_exp],
                         12: [z_silu], 15: [probsT_out, square], 17: [att_out], 20: [group_rstd]}
                if not is_last(g):
                    steps[13] = [next_bias, next_decays]
                return steps

            cut_chunk(z_chunk(0), part(group(0), 0))
            with act.Fori(0, SSM_G - 1) as g:
                cut_chunk(next_x(g), part(group(g), UPC))
                cut_chunk(next_z(g), joined(part(group(g), 2 * UPC), part(group(g + 1), 0)))

            def gate(ch, dst):
                wait_full(ch)
                act.activation(dst, acc[ch.bank][:, :, :], ACT.Sigmoid).then_inc(chunk_free[ch.bank], 1)

            def cut_y(part):
                if part == 0:
                    act.wait_ge(y_out, 4 * (SSM_G - 1))
                    act.wait_ge(shifted, 2 * SSM_G)
                    act.wait_ge(mix_ready, 2 * SSM_G)
                if part == 6:
                    act.wait_ge(gated, SSM_G)
                if part == 7:
                    act.wait_ge(y_out, 4 * SSM_G)
                if part < 8:
                    dst, src = y_hi[:, cut_at(part, 4), :], y32[:, cut_at(part, 4), :]
                else:
                    dst, src = att_hi[:, cut_at(part - 8, 4), :], qatt[:, cut_at(part - 8, 4), :]
                act.activation(dst, src, ACT.Copy).then_inc(y_hi_done, 1)

            cut_chunk(ga_chunk(0), joined(part(group(SSM_G - 1), UPC), {u: [lambda u=u: cut_y(u - 4)] for u in range(4, 8)}))
            cut_chunk(gb_chunk(0), joined(part(group(SSM_G - 1), 2 * UPC), {
                3: [lambda: gate(ga_chunk(0), sga[:, :, :])],
                5: [lambda: cut_y(4)], 6: [lambda: cut_y(5)], 7: [lambda: cut_y(6)]}))
            for p in range(7, 12):
                cut_y(p)

            def merge_gates(j):
                cut_chunk(ssm_chunk(j), {3: [lambda: gate(gb_chunk(j), sgb[:, :, :])]})
                cut_chunk(att_chunk(j))
                cut_chunk(next_ga(j))

                def gate_a():
                    act.wait_ge(chunk_free[0], ssm_chunk(j).left.val())
                    gate(next_ga(j), sga[:, :, :])

                def sgb_used():
                    act.wait_ge(mg_done, at(2, 2, j).val())
                cut_chunk(next_gb(j), {3: [gate_a], 7: [sgb_used]})

            with act.Fori(0, 3) as j:
                merge_gates(j)

            def merged_part(j):
                return [lambda: stationary(1, (2 * j, 2 * j + 1), None, st_hi)]

            def load_h():
                wait_full(ssm_chunk(3))
                for b in range(TB):
                    act.dma_start(h_tm[:, b, :], x[b * P:(b + 1) * P, :]).then_inc(h_loaded, 16)

            cut_chunk(ssm_chunk(3), {3: [lambda: gate(gb_chunk(3), sgb[:, :, :])], 7: merged_part(0), 10: merged_part(1), 13: merged_part(2)})
            cut_chunk(att_chunk(3), {3: [load_h]})

            def row_squares(before, ch, j, unread):
                act.wait_ge(chunk_free[ch.bank], ch.left.val())
                for b in range(TB):
                    squares(before + b, unread, h_tm[:, b, cut_at(j, CW)], b, j)

            def h_squares(j):
                return [lambda: row_squares((2 + j) * TB, out_chunk(j), j, hT_hi[:, 0:2, :].rearrange("p j t -> p (j t)"))]

            def h_part(j):
                return [lambda: stationary(2, (2 * j, 2 * j + 1), C_N2, up_hi)]

            cut_chunk(out_chunk(0), {7: merged_part(3)})
            for j in range(1, 4):
                cut_chunk(out_chunk(j), {4: h_squares(j - 1), 7: h_part(j - 1)})

            def relu_steps(half, j, pair=None):
                ch = up_chunk(half, j, pair)
                q = at(j, 8, half)
                tiles = cut_at(j, 4)
                if pair is not None:
                    q = q.along(2, pair)
                    tiles = bass.ds(pair * 8 + 4 * j, 4)

                def relu_():
                    wait_full(ch)
                    act.activation(relu[:, :, :], banks(ch), ACT.Relu).then_inc(chunk_free[ch.bank], 1)
                    act.wait_ge(chunk_free[ch.bank], ch.left.val())

                def square_():
                    act.activation(relu2[:, :, :], relu[:, :, :], ACT.Square).then_inc(relu_sq, 1)
                    act.wait_ge(relu_sq, (q + 1).val())

                def hi_():
                    act.activation(hT_hi[:, tiles, :], relu2[:, :, :], ACT.Copy).then_inc(hT_hi_done, 1)

                def lo_done():
                    act.wait_ge(hT_lo_done, (q + 1).val())
                return {3: [relu_], 4: [square_], 5: [hi_], 7: [lo_done]}

            def load_fw():
                wait_full(out_chunk(3))
                act.dma_start(fw[:, :], fnorm.partition_broadcast(P)).then_inc(fw_loaded, 16)

            def out_squares(j):
                return [lambda: row_squares((6 + j) * TB, down_chunk(1, j), j, relu2[:, 0:2, :].rearrange("p j t -> p (j t)"))]

            for half in range(2):
                cut_chunk(up_chunk(half, 0), {3: [load_fw], 4: h_squares(3), 5: [lambda: square_root(1)], 7: h_part(3)}
                          if half == 0 else None)
                with act.Fori(0, 3) as pair:
                    cut_chunk(up_chunk(half, 1, pair), relu_steps(half, 0, pair))
                    cut_chunk(up_chunk(half, 2, pair), relu_steps(half, 1, pair))
                cut_chunk(up_chunk(half, 7), relu_steps(half, 6))
                cut_chunk(down_chunk(half, 0), relu_steps(half, 7))
                for j in range(1, 4):
                    cut_chunk(down_chunk(half, j), {4: out_squares(j - 1)} if half == 1 else None)
            out_squares(3)[0]()
            square_root(2)
            act.wait_ge(rstd_ready, 3)
            act.wait_ge(fw_applied, 3 * TB)
            for cs in MAIN:
                act.activation(out_sb[:, 0, cs], out_sb[:, 0, cs], ACT.Copy, scale=rstd[:, 0:1]).then_inc(out_ready_act, 1)

        @block.vector
        def _(dve):
            def cut(n, count, steps=None):
                for u in range(count):
                    for run in (steps or {}).get(u, ()):
                        run()
                    m = n + u
                    slot = m.mod(RING)
                    dve.wait_ge(hi_ready, (m + 1).val())
                    dve.tensor_tensor(w_lo[:, slot, :], raw[:, slot, :], w_hi[:, slot, :], ALU.subtract).then_inc(lo_ready, 1)

            def wait_full(ch):
                dve.wait_ge(unit_used, ch.end.val())

            def cut_chunk(ch, steps=None):
                cut(ch.unit, ch.units, steps)

            def mean_squares(r, parts, count):
                dve.wait_ge(ss_ready, count)
                dve.tensor_reduce(ms, sums[:, :, 0:parts], AX.X, ALU.add).then_inc(stat_step, 1)
                dve.wait_ge(stat_step, 6 * r + 1)
                dve.tensor_scalar(ms, ms, 1.0 / D, EPS, ALU.mult, ALU.add).then_inc(stat_step, 1)

            def reciprocal_root(r):
                dve.wait_ge(root_ready, r + 1)
                dve.reciprocal(rstd_1, root).then_inc(stat_step, 1)
                dve.wait_ge(stat_step, 6 * r + 3)
                for b in range(TB):
                    y0 = rstd_1[:, b:b + 1]
                    dve.tensor_scalar(newton[:, b:b + 1], y0, y0, ms[:, b:b + 1], ALU.mult, ALU.mult).then_inc(stat_step, 1)
                dve.wait_ge(stat_step, 6 * r + 5)
                dve.tensor_scalar(newton, newton, -0.5, 1.5, ALU.mult, ALU.add).then_inc(stat_step, 1)
                dve.wait_ge(stat_step, 6 * r + 6)
                dve.tensor_tensor(rstd, rstd_1, newton, ALU.mult).then_inc(rstd_ready, 1)
                dve.wait_ge(rstd_ready, r + 1)

            def stationary(r, kps, wcol, hi, lo):
                for kp in kps:
                    dve.wait_ge(st_hi_done, KT * r + 2 * kp + 2)
                    for j in range(2):
                        k = 2 * kp + j
                        src = mp[:, kp % 4, j * T:(j + 1) * T]
                        scale = 1.0 if wcol is None else cols[:, wcol + k:wcol + k + 1]
                        dve.scalar_tensor_tensor(lo[:, k, :], src, scale, hi[:, k, :],
                                                 ALU.mult, ALU.subtract).then_inc(st_lo_done, 1)

            mean_squares(0, 2, 2 * TB)
            reciprocal_root(0)
            for half, b in ((0, 1), (1, 0), (1, 1)):
                xs = x_tm[:, b, cut_at(half, D // 2)]
                dve.tensor_scalar(xs, xs, rstd[:, b:b + 1], None, ALU.mult).then_inc(x_scaled[half], 1)
            dve.wait_ge(small_loaded, 32)
            cut(Lin(0), 1)
            stationary(0, range(0, 7), C_N1, st_hi, st_lo)
            cut(Lin(1), 1)
            stationary(0, range(7, 8), C_N1, st_hi, st_lo)

            def step(ins, s, count):
                ins.then_inc(s, 1)
                dve.wait_ge(s, count)

            def dt_a():
                dve.wait_ge(dt_act, 2)
                v = dtw[:, 0, :]
                step(dve.tensor_scalar(dtw[:, 1, :], v, -1.0, None, ALU.mult), dt_step, 1)
                step(dve.tensor_tensor(dtw[:, 1, :], v, dtw[:, 1, :], ALU.min), dt_step, 2)

            def dt_b():
                dve.wait_ge(dt_act, 3)
                step(dve.tensor_scalar(dtw[:, 3, :], dtw[:, 2, :], 1.0, None, ALU.add), dt_step, 3)

            def dt_c():
                step(dve.tensor_scalar(dtw[:, 5, :], dtw[:, 3, :], -1.0, None, ALU.add), dt_step, 4)
                step(dve.tensor_scalar(dtw[:, 6, :], dtw[:, 5, :], 0.0, None, ALU.is_equal), dt_step, 5)
                step(dve.tensor_tensor(dtw[:, 5, :], dtw[:, 5, :], dtw[:, 6, :], ALU.add), dt_step, 6)
                step(dve.reciprocal(dtw[:, 5, :], dtw[:, 5, :]), dt_step, 7)
                dve.wait_ge(dt_act, 4)
                step(dve.tensor_tensor(dtw[:, 6, :], dtw[:, 6, :], dtw[:, 4, :], ALU.add), dt_step, 8)
                step(dve.tensor_tensor(dtw[:, 6, :], dtw[:, 6, :], dtw[:, 5, :], ALU.mult), dt_step, 9)
                step(dve.tensor_tensor(dtw[:, 6, :], dtw[:, 6, :], dtw[:, 2, :], ALU.mult), dt_step, 10)
                step(dve.scalar_tensor_tensor(dtw[:, 8, :], dtw[:, 0, :], 0.0, dtw[:, 6, :], ALU.max, ALU.add), dt_step, 11)
                step(dve.tensor_scalar(dtw[:, 9, :], dtw[:, 8, :], smx[0:SSM_H, 0, 0:1], -1.0, ALU.mult, ALU.mult), dt_step, 12)

            def double(first):
                for i in range(first, first + 3):
                    s = 1 << i
                    src, dst = (9, 7) if i % 2 == 0 else (7, 9)
                    a = dtw[:, src, :].rearrange("h (c l) -> h c l", l=L)
                    b = dtw[:, dst, :].rearrange("h (c l) -> h c l", l=L)
                    dve.tensor_tensor(b[:, :, s:], a[:, :, s:], a[:, :, :L - s], ALU.add).then_inc(dt_step, 1)
                    step(dve.tensor_copy(b[:, :, :s], a[:, :, :s]), dt_step, 12 + 2 * (i + 1))

            def decay_sums():
                n = 24
                acs = dtw[:, 9, :].rearrange("h (c l) -> h c l", l=L)
                tot = [acs[:, c, L - 1:L] for c in range(NCH)]
                s01, s12, s012 = smx[0:SSM_H, 2, 0:1], smx[0:SSM_H, 2, 1:2], smx[0:SSM_H, 2, 2:3]
                dve.tensor_tensor(s01, tot[0], tot[1], ALU.add).then_inc(dt_step, 1)
                dve.tensor_tensor(s12, tot[1], tot[2], ALU.add).then_inc(dt_step, 1)
                n += 2
                dve.wait_ge(dt_step, n)
                step(dve.tensor_tensor(s012, s01, tot[2], ALU.add), dt_step, n + 1)
                n += 1
                rows = dtw[:, 10:13, :].rearrange("h a t -> h (a t)")
                lower, upper = rows[:, 0:SW].rearrange("h (c l) -> h c l", l=L), rows[:, SW:2 * SW].rearrange("h (c l) -> h c l", l=L)

                def put(dst, c, add, last=False):
                    if c is None:
                        ins = dve.memset(dst, 0.0)
                    elif add is None:
                        ins = dve.tensor_copy(dst, acs[:, c, :])
                    else:
                        ins = dve.tensor_scalar(dst, acs[:, c, :], add, None, ALU.add)
                    ins.then_inc(dt_ready if last else dt_step, 1)
                for k, (c, add) in enumerate([(0, None), (1, tot[0]), (2, s01), (3, s012), (2, None), (3, tot[2])]):
                    put(lower[:, k, :], c, add)
                for k, (c, add) in enumerate([(None, None), (1, None), (2, tot[1]), (3, s12), (None, None), (3, None)]):
                    put(upper[:, k, :], c, add, last=(k == 5))

            def dt_columns():
                dve.wait_ge(dtT_done, 1)
                dve.tensor_copy(tmcols[:, :, :], mp[:, 2, 0:4 * SSM_H].rearrange("p (a h) -> p a h", a=4)).then_inc(tmcols_ready, 1)

            cut_chunk(K_CHUNK, {5: [dt_a], 7: [dt_b]})
            cut_chunk(V_CHUNK, {2: [dt_c], 4: [lambda: double(0)], 6: [lambda: double(3)]})
            cut_chunk(bc_chunk(0), {0: [decay_sums], 6: [dt_columns]})

            def conv(k, tile0, ch):
                def half(t0):
                    def run():
                        if t0 == 0:
                            dve.wait_ge(chunk_free[ch.bank], ch.left.val())
                        base = k.times(15) + (4 * t0)
                        for tap in range(4):
                            for t in (t0, t0 + 1):
                                src = xraw[:, t, tap:tap + T]
                                wt = tile0 * 4 + (4 * t + C_CONVW + tap)
                                wcol = cols[:, cut_at(wt, 1)]
                                if tap == 0:
                                    ins = dve.tensor_scalar(xc[:, t, :], src, wcol, cols[:, cut_at(tile0 + (t + C_CONVB), 1)],
                                                            ALU.mult, ALU.add)
                                else:
                                    dve.wait_ge(conv_step, (base + (2 * (tap - 1) + (t - t0) + 1)).val())
                                    ins = dve.scalar_tensor_tensor(xc[:, t, :], src, wcol, xc[:, t, :], ALU.mult, ALU.add)
                                ins.then_inc(conv_done if (tap, t) == (3, 3) else conv_step, 1)
                    return run
                return [half(0)], [half(2)]

            for j in range(1, 4):
                a, b = conv(Lin(j - 1), DI // P + 4 * (j - 1), bc_chunk(j - 1))
                cut_chunk(bc_chunk(j), {4: a, 5: b})
            a, b = conv(Lin(3), DI // P + 12, bc_chunk(3))
            cut_chunk(q_chunk(0), {4: a, 5: b})

            def mask_cb(g):
                dve.wait_ge(cb_done, g + 1)
                dve.tensor_tensor(cbm[:, g, :], mp[:, g % 4, 0:SW], mask, ALU.mult).then_inc(cbm_ready, 1)

            cut_chunk(q_chunk(1), {5: [lambda: mask_cb(0), lambda: mask_cb(1)], 6: [lambda: mask_cb(2), lambda: mask_cb(3)]})
            cut_chunk(q_chunk(2), {3: [lambda: mask_cb(4), lambda: mask_cb(5)], 4: [lambda: mask_cb(6), lambda: mask_cb(7)]})
            cut_chunk(q_chunk(3))
            cut_chunk(x_chunk(0))

            def group(g):
                it = at(0, 1, g)
                z = z_chunk(g)
                sm = it.times(7)
                pr = probs[:, :, :].rearrange("p b (h k) -> p (b h) k", k=WIN)
                mx, less, den, rec = (smx[:, n, :] for n in range(4))
                sk = spread(cols[:, cut_at_off(g, 2, C_SINK)], (1, 2), (0, NCH))
                mx2 = mx.rearrange("p (e c) -> p e c", e=2)

                def softmax_max():
                    dve.wait_ge(scores_done, (it + 1).val())
                    dve.wait_ge(bias_loaded, at(32, 32, g).val())
                    dve.tensor_tensor(probs[:, :, :].rearrange("p e (c k) -> p e c k", k=WIN),
                                      mp[:, 0:2, :].rearrange("p e (c k) -> p e c k", k=WIN),
                                      spread(bias_g[:, :, :], (WIN, 2), (0, NCH), (1, WIN)), ALU.add).then_inc(sm_step, 1)
                    dve.wait_ge(sm_step, (sm + 1).val())
                    dve.memset(probs[:, :, 0:L], MASKED).then_inc(sm_step, 1)
                    dve.wait_ge(sm_step, (sm + 2).val())
                    dve.tensor_reduce(mx, pr, AX.X, ALU.max).then_inc(sm_step, 1)
                    dve.wait_ge(sm_step, (sm + 3).val())
                    dve.tensor_tensor(mx2, mx2, sk, ALU.max).then_inc(sm_step, 1)

                def softmax_shift():
                    dve.wait_ge(sm_step, (sm + 4).val())
                    dve.tensor_tensor(less.rearrange("p (e c) -> p e c", e=2), sk, mx2, ALU.subtract).then_inc(shifted, 1)
                    dve.tensor_tensor(pr, pr, spread(mx, (1, 8), (0, WIN)), ALU.subtract).then_inc(shifted, 1)

                def softmax_sum():
                    dve.wait_ge(exped, (it.times(2) + 2).val())
                    dve.tensor_reduce(den, pr, AX.X, ALU.add).then_inc(sm_step, 1)
                    dve.wait_ge(sm_step, (sm + 5).val())
                    dve.tensor_tensor(den, den, less, ALU.add).then_inc(sm_step, 1)
                    dve.wait_ge(sm_step, (sm + 6).val())
                    dve.reciprocal(rec, den).then_inc(sm_step, 1)

                def softmax_scale():
                    dve.wait_ge(sm_step, (sm + 7).val())
                    dve.tensor_tensor(pr, pr, spread(rec, (1, 8), (0, WIN)), ALU.mult).then_inc(probs_ready, 1)

                def times_dt():
                    dve.wait_ge(xT_done, (it + 1).val())
                    for blk in range(TB):
                        dts = spread(tmcols[:, blk, cut_at(g, HPG)], (1, HPG), (0, HD))
                        dve.tensor_tensor(xdt[:, blk, :].rearrange("p (h d) -> p h d", d=HD),
                                          mp[:, 2 + blk, :].rearrange("p (h d) -> p h d", d=HD), dts, ALU.mult).then_inc(xdt_ready, 1)

                yg = y32[:, cut_at(g, 4), :]

                def add_skip():
                    dve.wait_ge(y_done, (it + 1).val())
                    dve.wait_ge(silu_done, (it + 5).val())
                    for t in range(4):
                        src = mp[:, 2 + t // 2, (t % 2) * T:(t % 2 + 1) * T]
                        dve.scalar_tensor_tensor(yg[:, t, :], x_fm[:, t, :], cols[:, cut_at(g * 4 + (C_SKIP + t), 1)], src,
                                                 ALU.mult, ALU.add).then_inc(gate_step, 1)

                def gate():
                    dve.wait_ge(chunk_free[1], z.left.val())
                    dve.wait_ge(gate_step, at(4, 4, g).val())
                    dve.tensor_tensor(yg, yg, zs[:, :, :], ALU.mult).then_inc(gated, 1)

                def mean_square():
                    dve.wait_ge(sumsq_done, (it + 1).val())
                    dve.tensor_scalar(ms_g, mp[:, 1, 0:T], 1.0 / (4 * P), EPS, ALU.mult, ALU.add).then_inc(ms_ready, 1)

                def normalise():
                    gn = it.times(4)
                    y0, ms, t_ = rstd_g, ms_g, sq[:, 0, :]
                    dve.wait_ge(rstd0_ready, (it + 1).val())
                    dve.tensor_tensor(t_, y0, y0, ALU.mult).then_inc(gn_step, 1)
                    dve.wait_ge(gn_step, (gn + 1).val())
                    dve.tensor_tensor(t_, t_, ms, ALU.mult).then_inc(gn_step, 1)
                    dve.wait_ge(gn_step, (gn + 2).val())
                    dve.tensor_scalar(t_, t_, -0.5, 1.5, ALU.mult, ALU.add).then_inc(gn_step, 1)
                    dve.wait_ge(gn_step, (gn + 3).val())
                    dve.tensor_tensor(t_, y0, t_, ALU.mult).then_inc(gn_step, 1)
                    dve.wait_ge(gn_step, (gn + 4).val())
                    for t in range(4):
                        dve.scalar_tensor_tensor(yg[:, t, :], yg[:, t, :], cols[:, cut_at(g * 4 + (C_SSMN + t), 1)], t_,
                                                 ALU.mult, ALU.mult).then_inc(y_out, 1)

                def scales_read():
                    dve.wait_ge(y_out, at(4, 4, g).val())

                a, b = conv(it + 4, g * 4, x_chunk(g))
                return {4: a, 5: b, 8: [times_dt], 9: [softmax_max], 10: [softmax_shift], 12: [softmax_sum],
                        13: [softmax_scale, add_skip], 14: [gate], 18: [mean_square], 22: [normalise],
                        23: [scales_read]}

            cut_chunk(z_chunk(0), part(group(0), 0))
            with dve.Fori(0, SSM_G - 1) as g:
                cut_chunk(next_x(g), part(group(g), UPC))
                cut_chunk(next_z(g), joined(part(group(g), 2 * UPC), part(group(g + 1), 0)))

            def cut_y(p):
                dve.wait_ge(y_hi_done, p + 1)
                s = cut_at(p, 4)
                dve.tensor_tensor(y_lo[:, s, :], y32[:, s, :], y_hi[:, s, :], ALU.subtract).then_inc(y_lo_done, 1)

            cut_chunk(ga_chunk(0), joined(part(group(SSM_G - 1), UPC), {6: [lambda: cut_y(0)], 7: [lambda: cut_y(1)]}))
            cut_chunk(gb_chunk(0), joined(part(group(SSM_G - 1), 2 * UPC), {
                0: [lambda: cut_y(2)], 1: [lambda: cut_y(3)], 5: [lambda: cut_y(4)], 7: [lambda: cut_y(5)]}))
            cut_y(6)
            cut_y(7)

            def merge(j, last):
                ssm, att = ssm_chunk(j), att_chunk(j)

                def mcols(b):
                    return merged[:, b, cut_at(j, CW)]

                def ssm_part():
                    wait_full(ssm)
                    dve.wait_ge(chunk_free[0], ssm.turn.val())
                    for b in range(TB):
                        dve.tensor_tensor(mcols(b), acc[0][:, b, :], sga[:, b, :], ALU.mult).then_inc(mg_step if b == 0 else chunk_free[0], 1)

                def att_part():
                    wait_full(att)
                    dve.wait_ge(chunk_free[1], att.turn.val())
                    for b in range(TB):
                        dve.tensor_tensor(sgb[:, b, :], acc[1][:, b, :], sgb[:, b, :], ALU.mult).then_inc(mg_step if b == 0 else chunk_free[1], 1)
                    dve.wait_ge(chunk_free[0], ssm.left.val())
                    dve.wait_ge(chunk_free[1], att.left.val())
                    for b in range(TB):
                        dve.tensor_tensor(mcols(b), mcols(b), sgb[:, b, :], ALU.add).then_inc(mg_done, 1)
                if last:
                    def merged_part(n):
                        return [lambda: stationary(1, (2 * n, 2 * n + 1), None, st_hi, st_lo)]

                    cut_chunk(ssm, {7: merged_part(0), 10: merged_part(1), 13: merged_part(2)})
                    cut_chunk(att, {3: [ssm_part]})
                    cut_chunk(out_chunk(0), {3: [att_part], 7: merged_part(3)})
                else:
                    cut_chunk(ssm)
                    cut_chunk(att, {3: [ssm_part]})
                    cut_chunk(next_ga(j), {3: [att_part]})
                    cut_chunk(next_gb(j))

            with dve.Fori(0, 3) as j:
                merge(j, False)
            merge(3, True)

            def add_to_h(ch, j):
                wait_full(ch)
                for b in range(TB):
                    hs = h_tm[:, b, j * CW:(j + 1) * CW]
                    dve.tensor_tensor(hs, hs, acc[ch.bank][:, b, :], ALU.add).then_inc(h_step if b == 0 else chunk_free[ch.bank], 1)

            def h_part(j):
                return [lambda: stationary(2, (2 * j, 2 * j + 1), C_N2, up_hi, up_lo)]

            dve.wait_ge(h_loaded, 32)
            for j in range(1, 4):
                cut_chunk(out_chunk(j), {3: [lambda: add_to_h(out_chunk(j - 1), j - 1)], 7: h_part(j - 1)})

            def norm_2():
                reciprocal_root(1)
                dve.tensor_tensor(rstd_sq, rstd, rstd, ALU.mult).then_inc(rstd_sq_ready, 1)
                dve.wait_ge(rstd_sq_ready, 1)

            def add_mlp(half, j):
                ch = down_chunk(half, j)

                def run():
                    wait_full(ch)
                    for b in range(TB):
                        hs = h_tm[:, b, j * CW:(j + 1) * CW]
                        dve.scalar_tensor_tensor(hs, acc[ch.bank][:, b, :], rstd_sq[:, b:b + 1], hs,
                                                 ALU.mult, ALU.add).then_inc(h_step if b == 0 else chunk_free[ch.bank], 1)
                return [run]

            def cut_h(half, j, pair=None):
                q = at(j, 8, half)
                tiles = cut_at(j, 4)
                if pair is not None:
                    q = q.along(2, pair)
                    tiles = bass.ds(pair * 8 + 4 * j, 4)

                def run():
                    dve.wait_ge(hT_hi_done, (q + 1).val())
                    dve.tensor_tensor(hT_lo[:, tiles, :], relu2[:, :, :], hT_hi[:, tiles, :], ALU.subtract).then_inc(hT_lo_done, 1)
                return {6: [run]}

            for half in range(2):
                if half == 0:
                    cut_chunk(up_chunk(0, 0), {3: [lambda: add_to_h(out_chunk(3), 3)], 5: [lambda: mean_squares(1, 4, 6 * TB)],
                                               6: [norm_2], 7: h_part(3)})
                else:
                    cut_chunk(up_chunk(1, 0), {3: add_mlp(0, 3)})
                with dve.Fori(0, 3) as pair:
                    cut_chunk(up_chunk(half, 1, pair), cut_h(half, 0, pair))
                    cut_chunk(up_chunk(half, 2, pair), cut_h(half, 1, pair))
                cut_chunk(up_chunk(half, 7), cut_h(half, 6))
                cut_chunk(down_chunk(half, 0), cut_h(half, 7))
                for j in range(1, 4):
                    cut_chunk(down_chunk(half, j), {3: add_mlp(half, j - 1)})
            add_mlp(1, 3)[0]()
            mean_squares(2, 4, 10 * TB)
            reciprocal_root(2)
            dve.wait_ge(fw_loaded, 16)
            for b in range(TB):
                dve.scalar_tensor_tensor(out_sb[:, b, LAST], h_tm[:, b, LAST], rstd[:, b:b + 1], fw[:, LAST],
                                         ALU.mult, ALU.mult).then_inc(out_ready_dve, 1)
            dve.wait_ge(fw_applied, 3 * TB)
            for cs in MAIN:
                dve.tensor_scalar(out_sb[:, 1, cs], out_sb[:, 1, cs], rstd[:, 1:2], None, ALU.mult).then_inc(out_ready_dve, 1)

        @block.tensor
        def _(pe):
            def start_chunk(ch):
                if ch.turn.c > 0:
                    pe.wait_ge(chunk_free[ch.bank], ch.turn.val())

            def token_major(ch, hi, lo, steps=None):
                nk = ch.units * KPU
                start_chunk(ch)
                for u in range(ch.units):
                    for run in (steps or {}).get(u, ()):
                        run()
                    m = ch.unit + u
                    slot = m.mod(RING)
                    pe.wait_ge(lo_ready, (m + 1).val())
                    for kk in range(KPU):
                        k = u * KPU + kk
                        wh, wl = (w[:, slot, kk * CW:(kk + 1) * CW] for w in (w_hi, w_lo))
                        for b in range(TB):
                            bs = slice(b * P, (b + 1) * P)
                            o = acc[ch.bank][:, b, :]
                            pe.matmul(o, hi[:, k, bs], wh, start=(k == 0), stop=False)
                            pe.matmul(o, hi[:, k, bs], wl, start=False, stop=False)
                            mm = pe.matmul(o, lo[:, k, bs], wh, start=False, stop=(k == nk - 1))
                    mm.then_inc(unit_used, 1)

            def feature_major(ch, steps=None, hi=st_hi, lo=st_lo):
                start_chunk(ch)
                for u in range(ch.units):
                    for run in (steps or {}).get(u, ()):
                        run()
                    m = ch.unit + u
                    slot = m.mod(RING)
                    pe.wait_ge(lo_ready, (m + 1).val())
                    for kk in range(KPU):
                        k = u * KPU + kk
                        for t in range(4):
                            ws = slice(kk * CW + t * P, kk * CW + (t + 1) * P)
                            o = acc[ch.bank][:, t // 2, (t % 2) * T:(t % 2 + 1) * T]
                            pe.matmul(o, w_hi[:, slot, ws], hi[:, k, :], start=(k == 0 and t % 2 == 0), stop=False, skip_group_check=True)
                            pe.matmul(o, w_hi[:, slot, ws], lo[:, k, :], start=False, stop=False, skip_group_check=True)
                            mm = pe.matmul(o, w_lo[:, slot, ws], hi[:, k, :], start=False, stop=(k == KT - 1), skip_group_check=True)
                    mm.then_inc(unit_used, 1)

            def transposes(r, kps, src):
                for kp in kps:
                    if kp >= 4:
                        pe.wait_ge(st_lo_done, KT * r + 2 * (kp - 3))
                    for j in range(2):
                        for b in range(TB):
                            k = 2 * kp + j
                            mm = pe.transpose(mp[:, kp % 4, j * T + b * P:j * T + (b + 1) * P], src[:, b, k * P:(k + 1) * P], ident)
                    mm.then_inc(tr_done, 1)

            pe.wait_ge(small_loaded, 32)
            for half in range(2):
                pe.wait_ge(x_scaled[half], TB)
                transposes(0, range(4 * half, 4 * half + 4), x_tm)

            for u in range(DT_UNITS):
                pe.wait_ge(st_lo_done, (u + 1) * KT // DT_UNITS)
                pe.wait_ge(lo_ready, u + 1)
                for kk in range(UE // P):
                    k = u * (UE // P) + kk
                    ws = slice(kk * P, (kk + 1) * P)
                    o = acc[1][:, 0, 0:T]
                    pe.matmul(o, w_hi[:, u, ws], st_hi[:, k, :], start=(k == 0), stop=False)
                    pe.matmul(o, w_hi[:, u, ws], st_lo[:, k, :], start=False, stop=False)
                    mm = pe.matmul(o, w_lo[:, u, ws], st_hi[:, k, :], start=False, stop=(k == KT - 1))
                mm.then_inc(unit_used, 1)
            pe.wait_ge(table_loaded, 32)
            pe.matmul(mp[0:ATT_H, 3, 0:LINE], relt_sb, onehot_sb, start=True, stop=True).then_inc(line_done, 1)

            feature_major(K_CHUNK)

            def dt_transposes():
                pe.wait_ge(dt_ready, 1)
                for n, tile in enumerate((8, 9)):
                    for blk in range(TB):
                        mm = pe.transpose(mp[:, 2, (2 * n + blk) * SSM_H:(2 * n + blk + 1) * SSM_H],
                                          dtw[:, tile, blk * P:(blk + 1) * P], ident[0:SSM_H, 0:SSM_H])
                mm.then_inc(dtT_done, 1)

            pe.wait_ge(dt_act, 1)
            token_major(V_CHUNK, st_hi, st_lo)
            feature_major(bc_chunk(0), {3: [dt_transposes]})
            for j in range(1, 4):
                feature_major(bc_chunk(j))
            feature_major(q_chunk(0))

            def cb_products(groups):
                def run():
                    pe.wait_ge(silu_done, 4)
                    pe.wait_ge(tmcols_ready, 1)
                    pe.wait_ge(line_copied, 1)
                    for g in groups:
                        if g >= 4:
                            pe.wait_ge(cbm_ready, g - 3)
                        b_, c_ = bc[:, g, :], bc[:, SSM_G + g, :]
                        pe.matmul(mp[:, g % 4, 0:T], b_[:, 0:P], c_, start=True, stop=True)
                        pe.matmul(mp[:, g % 4, T:SW], b_[:, P:T], c_[:, P:T], start=True, stop=True).then_inc(cb_done, 1)
                return [run]

            feature_major(q_chunk(1), {1: cb_products(range(4)), 6: cb_products(range(4, 8))})
            feature_major(q_chunk(2))
            feature_major(q_chunk(3))
            feature_major(x_chunk(0))
            pe.wait_ge(cbm_ready, SSM_G)

            def group(g):
                it = at(0, 1, g)

                def scores_ready():
                    pe.wait_ge(qkv_ready, at(3, 3, g).val())

                def scores():
                    for c in range(NCH):
                        for e in range(2):
                            ps = slice(e * HD, (e + 1) * HD)
                            mm = pe.matmul(mp[:, e, c * WIN:(c + 1) * WIN], q_g[ps, c, :], k_g[ps, c * L:c * L + WIN],
                                           start=True, stop=True)
                    mm.then_inc(scores_done, 1)

                def x_transposes():
                    pe.wait_ge(silu_done, (it + 5).val())
                    for blk in range(TB):
                        for t in range(4):
                            mm = pe.transpose(mp[:, 2 + blk, t * P:(t + 1) * P], x_fm[:, t, blk * P:(blk + 1) * P], ident)
                    mm.then_inc(xT_done, 1)

                def p_transposes():
                    pe.wait_ge(probs_ready, (it + 1).val())
                    for e in range(2):
                        for c in range(NCH):
                            cs = slice(c * WIN, (c + 1) * WIN)
                            mm = pe.transpose(mp[:, e, cs], probs[:, e, cs], ident)
                    mm.then_inc(pT_done, 1)

                def ssd():
                    pe.wait_ge(xdt_ready, at(2, 2, g).val())
                    pe.wait_ge(mix_ready, at(2, 2, g).val())
                    for h in range(HPG):
                        t, hp = h // 2, slice((h % 2) * HD, (h % 2 + 1) * HD)
                        hs = slice(h * HD, (h + 1) * HD)
                        d = dec[h // 4][:, h % 4, :]
                        o = mp[hp, 2 + t // 2, (t % 2) * T:(t % 2 + 1) * T]
                        pe.matmul(o, xdt[:, 0, hs], d[:, 0:T], start=True, stop=False)
                        mm = pe.matmul(o[:, P:T], xdt[:, 1, hs], d[:, T:SW], start=False, stop=True)
                    mm.then_inc(y_done, 1)

                def weighted_values():
                    pe.wait_ge(pT_copied, (it + 1).val())
                    for c in range(NCH):
                        for e in range(2):
                            o = mp[e * HD:(e + 1) * HD, 0, :].rearrange("p (t q) -> p t q", t=2)[:, :, c * L:(c + 1) * L]
                            pt = probsT[:, e, c * WIN:(c + 1) * WIN].rearrange("p (t q) -> p t q", t=2)
                            mm = pe.matmul(o, v_g[:, c, :], pt, start=True, stop=True)
                    mm.then_inc(pv_done, 1)

                def sums_of_squares():
                    pe.wait_ge(folded, (it + 1).val())
                    pe.matmul(mp[:, 1, 0:T], ones, sq[:, 0, :], start=True, stop=True).then_inc(sumsq_done, 1)

                def banks_read():
                    pe.wait_ge(att_copied, (it + 1).val())
                    pe.wait_ge(ms_ready, (it + 1).val())

                return {2: [scores_ready], 3: [scores], 5: [x_transposes], 8: [ssd], 11: [p_transposes], 13: [weighted_values],
                        14: [sums_of_squares], 18: [banks_read]}

            feature_major(z_chunk(0), part(group(0), 0))
            with pe.Fori(0, SSM_G - 1) as g:
                feature_major(next_x(g), part(group(g), UPC))
                feature_major(next_z(g), joined(part(group(g), 2 * UPC), part(group(g + 1), 0)))
            token_major(ga_chunk(0), st_hi, st_lo, part(group(SSM_G - 1), UPC))

            token_major(gb_chunk(0), st_hi, st_lo)

            def merge(j, last):
                cut_parts = {2 * p: [lambda p=p: pe.wait_ge(y_lo_done, p + 1)] for p in range(8)}
                if last:
                    def merged_part(n):
                        return [lambda: transposes(1, (2 * n, 2 * n + 1), merged)]
                    pe.wait_ge(mg_done, 6)
                    cut_parts = joined(cut_parts, {3: merged_part(0), 6: merged_part(1), 9: merged_part(2)})
                token_major(ssm_chunk(j), y_hi, y_lo, cut_parts)
                pe.wait_ge(att_lo_done, 4)
                token_major(att_chunk(j), att_hi, att_lo)
                if not last:
                    token_major(next_ga(j), st_hi, st_lo)
                    token_major(next_gb(j), st_hi, st_lo)

            with pe.Fori(0, 3) as j:
                merge(j, False)
            merge(3, True)

            def wait_lo(count):
                return [lambda: pe.wait_ge(st_lo_done, count)]

            def last_merged():
                pe.wait_ge(mg_done, 8)
                transposes(1, (6, 7), merged)

            def h_transposes(j):
                def run():
                    ch = out_chunk(j)
                    pe.wait_ge(chunk_free[ch.bank], ch.left.val())
                    transposes(2, (2 * j, 2 * j + 1), h_tm)
                return [run]

            token_major(out_chunk(0), st_hi, st_lo, {0: wait_lo(KT + 12), 3: [last_merged], 6: wait_lo(2 * KT)})
            for j in range(1, 4):
                token_major(out_chunk(j), st_hi, st_lo, {3: h_transposes(j - 1)})

            for half in range(2):
                feature_major(up_chunk(half, 0), {0: wait_lo(2 * KT + 12), 3: h_transposes(3), 6: wait_lo(3 * KT)}
                              if half == 0 else None, up_hi, up_lo)
                with pe.Fori(0, 3) as pair:
                    for j in range(1, 3):
                        feature_major(up_chunk(half, j, pair), None, up_hi, up_lo)
                feature_major(up_chunk(half, 7), None, up_hi, up_lo)

                def all_h():
                    pe.wait_ge(hT_lo_done, 8 * (half + 1))
                pe.wait_ge(hT_lo_done, 8 * half + 7)
                for j in range(4):
                    token_major(down_chunk(half, j), hT_hi, hT_lo, {14: [all_h]} if j == 0 else None)


def _t5_bucket(rel):
    nb = BUCKETS // 2
    ret = (rel > 0).astype(np.int32) * nb
    n = np.abs(rel)
    exact = nb // 2
    large = exact + (np.log(np.maximum(n, 1) / exact) / np.log(MAX_DIST / exact) * (nb - exact)).astype(np.int32)
    large = np.minimum(large, nb - 1)
    return (ret + np.where(n < exact, n, large)).astype(np.int32)


def kernel(x, rel_table, norm1_w, w_in, conv_w, conv_b, dt_bias, a_log, d_skip, ssm_norm_w, sinks,
           w_proj_ssm, w_proj_attn, w_out, norm2_w, w_up, w_down, final_norm_w):
    import concourse.bacc as _bacc
    from concourse.bass_utils import run_bass_kernel_spmd as _run

    def tiles(v):
        return np.asarray(v).reshape(-1, P).T

    def column(v):
        full = np.zeros((P, 1), np.float32)
        full[:SSM_H, 0] = np.asarray(v)
        return full

    cw = np.asarray(conv_w)[0].reshape(4, CONV_T, P).transpose(2, 1, 0).reshape(P, 4 * CONV_T)
    cols = np.concatenate([
        cw, tiles(conv_b[0]), tiles(norm1_w[0]), tiles(norm2_w[0]), tiles(ssm_norm_w[0]),
        tiles(np.repeat(np.asarray(d_skip)[0], HD)), np.repeat(np.asarray(sinks)[0].reshape(KV, 2, 2).transpose(1, 0, 2).reshape(2, 2 * KV), L, axis=0),
        column(dt_bias[0]), column(a_log[0])], axis=1)
    tri = np.triu(np.ones((P, P), np.float32))
    one = np.ones((P, P), np.float32)
    consts = np.concatenate([np.eye(P, dtype=np.float32), tri, one, tri, one], axis=1)
    onehot = np.zeros((BUCKETS, LINE), np.float32)
    rel = np.arange(LINE - 1) - (WIN - 1)
    onehot[_t5_bucket(rel), np.arange(LINE - 1)] = 1.0

    given = {
        "x": np.asarray(x)[0], "w_in": np.asarray(w_in)[0], "w_ssm": np.asarray(w_proj_ssm)[0],
        "w_att": np.asarray(w_proj_attn)[0], "w_out": np.asarray(w_out)[0], "w_up": np.asarray(w_up)[0],
        "w_down": np.asarray(w_down)[0], "rel_table": np.asarray(rel_table), "fnorm": np.asarray(final_norm_w),
        "cols_in": cols, "consts_in": consts, "onehot_in": onehot,
    }
    nc = _bacc.Bacc("TRN2", target_bir_lowering=False, num_devices=1)
    arrays, args = {}, []
    for name, a in given.items():
        a = np.ascontiguousarray(a)
        arrays[f"in_{name}"] = a
        args.append(nc.dram_tensor(f"in_{name}", a.shape, mybir.dt.from_np(a.dtype), kind="ExternalInput").ap())
    args.append(nc.dram_tensor("out_0", (T, D), F32, kind="ExternalOutput").ap())
    build(nc, *args)
    r = _run(nc, [arrays], core_ids=[0])
    return r.results[0]["out_0"].reshape(1, T, D)
```
